# Optimizing a Trainium2 kernel written in Bass

```python
import jax, jax.numpy as jnp
from jax import lax
import numpy as np
import math
import jax
import jax.numpy as jnp

D_MODEL = 1024
BATCH = 1
SEQ = 512
DEPTH = 1

GRID_W = 64
CTX_LEN = 256
N_MIXERS = 2
N_A_LAYERS = (DEPTH + N_MIXERS - 1) // N_MIXERS
N_B_LAYERS = DEPTH // N_MIXERS
POOL_WINDOWS = (2, 4, 8, 16)
POOL_GROUPS = 4
POOL_GROUP_DIM = D_MODEL // POOL_GROUPS
NA_HEADS = 16
NA_HEAD_DIM = D_MODEL // NA_HEADS
WIN_H = 8
WIN_W = 16
COL_BAND = 2 * WIN_W
D_FF = 2816
CONV_W = 3
ADA_CHUNKS = 6
EPS = 1e-6
NEG_INF = -1e30


def rms_norm(x, g):
    x32 = x.astype(jnp.float32)
    y = x32 * lax.rsqrt(jnp.mean(x32 * x32, axis=-1, keepdims=True) + EPS)
    return (y * g.astype(jnp.float32)).astype(x.dtype)

def modulate(h, shift, scale):
    return h * (1 + scale) + shift

def ada_mods(cond, w, b):
    mods = (jax.nn.silu(cond) @ w + b)[..., None, :]
    return jnp.split(mods, ADA_CHUNKS, axis=-1)

def centred_window_mean(u, w):
    n = u.shape[1]
    u32 = u.astype(jnp.float32)
    cs = jnp.concatenate([jnp.zeros_like(u32[:, :1]), jnp.cumsum(u32, axis=1)], axis=1)
    t = jnp.arange(n)
    lo = jnp.maximum(t - w // 2, 0)
    hi = jnp.minimum(t + w // 2, n)
    cnt = (hi - lo).astype(jnp.float32)
    return ((cs[:, hi] - cs[:, lo]) / cnt[None, :, None]).astype(u.dtype)

def pool_mixer(u, w_groups, scale):
    outs = []
    for g, win in enumerate(POOL_WINDOWS):
        ug = u[..., g * POOL_GROUP_DIM:(g + 1) * POOL_GROUP_DIM]
        outs.append((centred_window_mean(ug, win) - ug) @ w_groups[g])
    return jnp.concatenate(outs, axis=-1) * scale

def depthwise_conv(h, w, b):
    n = h.shape[1]
    p = CONV_W // 2
    hp = jnp.pad(h, ((0, 0), (p, p), (0, 0)))
    out = b
    for j in range(CONV_W):
        out = out + hp[:, j:j + n] * w[j]
    return out

def conv_ffn(u, w_up, conv_w, conv_b, w_down):
    h = depthwise_conv(u @ w_up, conv_w, conv_b)
    gate, val = jnp.split(h, 2, axis=-1)
    return (jax.nn.gelu(gate) * val) @ w_down

def column_band_tables():
    n_cb = GRID_W // WIN_W
    qcol = np.arange(GRID_W).reshape(n_cb, WIN_W)
    band_start = np.clip(np.arange(n_cb) * WIN_W - WIN_W // 2, 0, GRID_W - COL_BAND)
    band = band_start[:, None] + np.arange(COL_BAND)[None]
    win_start = np.clip(qcol - WIN_W // 2, 0, GRID_W - WIN_W)
    kc = band[:, None, :]
    valid = (kc >= win_start[..., None]) & (kc < win_start[..., None] + WIN_W)
    dc = np.clip(kc - qcol[..., None] + WIN_W - 1, 0, 2 * WIN_W - 2)
    return band, valid, dc

def split_heads(t, n_parts):
    bsz, n, _ = t.shape
    t = t.reshape(bsz, n, n_parts, NA_HEADS, NA_HEAD_DIM)
    return [jnp.transpose(t[:, :, j], (0, 2, 1, 3)) for j in range(n_parts)]

def context_self_attention(uc, w_qkv, w_o):
    bsz, m, _ = uc.shape
    q_c, k_c, v_c = split_heads(uc @ w_qkv, 3)
    s = jnp.einsum('bhqd,bhkd->bhqk', q_c, k_c).astype(jnp.float32) * (NA_HEAD_DIM ** -0.5)
    p = jax.nn.softmax(s, axis=-1).astype(v_c.dtype)
    o = jnp.einsum('bhqk,bhkd->bhqd', p, v_c)
    return jnp.transpose(o, (0, 2, 1, 3)).reshape(bsz, m, D_MODEL) @ w_o

def neighbourhood_attention(u, uc, w_qkv, w_o, rpb):
    bsz, n, _ = u.shape
    rows = n // GRID_W
    kh = min(WIN_H, rows)
    n_cb = GRID_W // WIN_W
    nk = kh * COL_BAND
    scale = NA_HEAD_DIM ** -0.5
    band, valid, dc = column_band_tables()
    band_idx = jnp.asarray(band)
    col_valid = jnp.asarray(valid)
    dc_idx = jnp.asarray(dc)

    q, k, v = [t.reshape(bsz, NA_HEADS, rows, GRID_W, NA_HEAD_DIM) for t in split_heads(u @ w_qkv, 3)]
    k_c, v_c = split_heads(uc @ w_qkv[:, D_MODEL:], 2)

    def row_block(r):
        s0 = jnp.clip(r - kh // 2, 0, rows - kh)
        q_r = lax.dynamic_index_in_dim(q, r, axis=2, keepdims=False)
        q_r = q_r.reshape(bsz, NA_HEADS, n_cb, WIN_W, NA_HEAD_DIM)

        def gather_band(t):
            t_r = lax.dynamic_slice_in_dim(t, s0, kh, axis=2)
            t_b = t_r[:, :, :, band_idx]
            return jnp.moveaxis(t_b, 3, 2).reshape(bsz, NA_HEADS, n_cb, nk, NA_HEAD_DIM)

        k_b, v_b = gather_band(k), gather_band(v)
        dr_idx = s0 + jnp.arange(kh) - r + WIN_H - 1
        bias = rpb[:, dr_idx[:, None, None, None], dc_idx[None]]
        bias = jnp.where(col_valid[None, None], bias.astype(jnp.float32), NEG_INF)
        bias = jnp.moveaxis(bias, 1, 3).reshape(NA_HEADS, n_cb, WIN_W, nk)
        s_lat = jnp.einsum('bhnqd,bhnkd->bhnqk', q_r, k_b).astype(jnp.float32) * scale + bias
        s_ctx = jnp.einsum('bhnqd,bhcd->bhnqc', q_r, k_c).astype(jnp.float32) * scale
        p = jax.nn.softmax(jnp.concatenate([s_lat, s_ctx], axis=-1), axis=-1).astype(v.dtype)
        o = (jnp.einsum('bhnqk,bhnkd->bhnqd', p[..., :nk], v_b)
             + jnp.einsum('bhnqc,bhcd->bhnqd', p[..., nk:], v_c))
        return o.reshape(bsz, NA_HEADS, GRID_W, NA_HEAD_DIM)

    o = lax.map(row_block, jnp.arange(rows))
    return jnp.transpose(o, (1, 0, 3, 2, 4)).reshape(bsz, n, D_MODEL) @ w_o

def first_inputs(seed: int = 0) -> dict:
    key = jax.random.key(seed)
    ks = jax.random.split(key, 19)
    D = D_MODEL
    G = POOL_GROUP_DIM

    def nrm(k, shape, s):
        return jax.random.normal(k, shape, jnp.float32) * s

    return {
        'x': nrm(ks[0], (BATCH, SEQ, D), 1.0),
        'c': nrm(ks[1], (BATCH, D), 1.0),
        'ctx': nrm(ks[2], (BATCH, CTX_LEN, D), 1.0),
        'c_ctx': nrm(ks[3], (D,), 1.0),
        'ada_w': nrm(ks[4], (DEPTH, D, ADA_CHUNKS * D), 0.5 * D ** -0.5),
        'ada_b': nrm(ks[5], (DEPTH, ADA_CHUNKS * D), 0.02),
        'mix_pre_g': 1.0 + nrm(ks[6], (DEPTH, D), 0.05),
        'mix_post_g': 1.0 + nrm(ks[7], (DEPTH, D), 0.05),
        'ffn_pre_g': 1.0 + nrm(ks[8], (DEPTH, D), 0.05),
        'ffn_post_g': 1.0 + nrm(ks[9], (DEPTH, D), 0.05),
        'pool_w': nrm(ks[10], (N_A_LAYERS, POOL_GROUPS, G, G), G ** -0.5),
        'pool_scale': 1.0 + nrm(ks[11], (N_A_LAYERS, D), 0.1),
        'na_w_qkv': nrm(ks[12], (N_B_LAYERS, D, 3 * D), D ** -0.5),
        'na_w_o': nrm(ks[13], (N_B_LAYERS, D, D), D ** -0.5),
        'na_rpb': nrm(ks[14], (N_B_LAYERS, NA_HEADS, 2 * WIN_H - 1, 2 * WIN_W - 1), 0.5),
        'ffn_w_up': nrm(ks[15], (DEPTH, D, 2 * D_FF), D ** -0.5),
        'ffn_conv_w': nrm(ks[16], (DEPTH, CONV_W, 2 * D_FF), CONV_W ** -0.5),
        'ffn_conv_b': nrm(ks[17], (DEPTH, 2 * D_FF), 0.02),
        'ffn_w_down': nrm(ks[18], (DEPTH, D_FF, D), D_FF ** -0.5),
    }

def first_block(x, c, ctx, c_ctx, ada_w, ada_b, mix_pre_g, mix_post_g, ffn_pre_g, ffn_post_g,
              pool_w, pool_scale, na_w_qkv, na_w_o, na_rpb,
              ffn_w_up, ffn_conv_w, ffn_conv_b, ffn_w_down):
    for i in range(DEPTH):
        last = i == DEPTH - 1
        j = i // N_MIXERS
        sh1, sc1, g1, sh2, sc2, g2 = ada_mods(c, ada_w[i], ada_b[i])
        csh1, csc1, cg1, csh2, csc2, cg2 = ada_mods(c_ctx, ada_w[i], ada_b[i])

        u = modulate(rms_norm(x, mix_pre_g[i]), sh1, sc1)
        if i % N_MIXERS == 0:
            y = pool_mixer(u, pool_w[j], pool_scale[j])
            if not last:
                uc = modulate(rms_norm(ctx, mix_pre_g[i]), csh1, csc1)
                yc = pool_mixer(uc, pool_w[j], pool_scale[j])
        else:
            uc = modulate(rms_norm(ctx, mix_pre_g[i]), csh1, csc1)
            y = neighbourhood_attention(u, uc, na_w_qkv[j], na_w_o[j], na_rpb[j])
            if not last:
                yc = context_self_attention(uc, na_w_qkv[j], na_w_o[j])
        x = x + g1 * rms_norm(y, mix_post_g[i])
        if not last:
            ctx = ctx + cg1 * rms_norm(yc, mix_post_g[i])

        f = conv_ffn(modulate(rms_norm(x, ffn_pre_g[i]), sh2, sc2),
                     ffn_w_up[i], ffn_conv_w[i], ffn_conv_b[i], ffn_w_down[i])
        x = x + g2 * rms_norm(f, ffn_post_g[i])
        if not last:
            fc = conv_ffn(modulate(rms_norm(ctx, ffn_pre_g[i]), csh2, csc2),
                          ffn_w_up[i], ffn_conv_w[i], ffn_conv_b[i], ffn_w_down[i])
            ctx = ctx + cg2 * rms_norm(fc, ffn_post_g[i])
    return x


DEPTH_2 = 2

CHUNK = 64
Q_BLOCK = 128
N_HEADS = 16
HEAD_DIM = 64
D_ATT = N_HEADS * HEAD_DIM
SSM_GROUP = 16
D_SSM = D_MODEL
N_GROUPS = D_SSM // SSM_GROUP
STATE = 64
_FF_RAW = -(-8 * D_MODEL // 3)
D_FF_2 = -(-_FF_RAW // 256) * 256
N_FOX = (DEPTH_2 + 1) // 2
N_S5 = DEPTH_2 // 2
DT_MIN = 1e-3
DT_MAX = 1e-1


def rmsnorm(x, gain):
    xf = x.astype(jnp.float32)
    y = xf * lax.rsqrt(jnp.mean(xf * xf, axis=-1, keepdims=True) + EPS)
    return (y * gain.astype(jnp.float32)).astype(x.dtype)

def fox_mixer(h, w_in, b_f, q_gain, k_gain, w_out):
    bsz, seq_len, _ = h.shape
    proj = h @ w_in
    q = proj[..., :D_ATT]
    k = proj[..., D_ATT:2 * D_ATT]
    v = proj[..., 2 * D_ATT:3 * D_ATT]
    gate = proj[..., 3 * D_ATT:4 * D_ATT]
    f_logit = proj[..., 4 * D_ATT:]

    def heads(t):
        return t.reshape(bsz, seq_len, N_HEADS, HEAD_DIM).transpose(0, 2, 1, 3)

    q = rmsnorm(heads(q), q_gain)
    k = rmsnorm(heads(k), k_gain)
    v = heads(v)
    log_f = jax.nn.log_sigmoid(f_logit.astype(jnp.float32) + b_f.astype(jnp.float32))
    c = jnp.cumsum(log_f, axis=1).transpose(0, 2, 1)
    scale = HEAD_DIM ** -0.5

    outs = []
    for blk in range(seq_len // Q_BLOCK):
        q0 = blk * Q_BLOCK
        k_end = q0 + Q_BLOCK
        qb = q[:, :, q0:k_end]
        kb = k[:, :, :k_end]
        vb = v[:, :, :k_end]
        s = jnp.einsum('bhqd,bhkd->bhqk', qb, kb).astype(jnp.float32) * scale
        s = s + c[:, :, q0:k_end, None] - c[:, :, None, :k_end]
        q_pos = q0 + jnp.arange(Q_BLOCK)
        mask = q_pos[:, None] >= jnp.arange(k_end)[None, :]
        s = jnp.where(mask, s, -jnp.inf)
        p = jax.nn.softmax(s, axis=-1).astype(vb.dtype)
        outs.append(jnp.einsum('bhqk,bhkd->bhqd', p, vb))
    o = jnp.concatenate(outs, axis=2)
    o = o.transpose(0, 2, 1, 3).reshape(bsz, seq_len, D_ATT)
    o = o * jax.nn.sigmoid(gate)
    return o @ w_out

def _complex_linear_combine(e1, e2):
    a1r, a1i, b1r, b1i = e1
    a2r, a2i, b2r, b2i = e2
    return (a2r * a1r - a2i * a1i,
            a2r * a1i + a2i * a1r,
            a2r * b1r - a2i * b1i + b2r,
            a2r * b1i + a2i * b1r + b2i)

def s5_mixer(h, w_in, log_dt, lam_re, lam_im, b_re, b_im, c_re, c_im, d_skip, w_glu, w_out):
    f32 = jnp.float32
    bsz, seq_len, _ = h.shape
    u = (h @ w_in).astype(f32)
    lam_re = lam_re.astype(f32)
    lam_im = lam_im.astype(f32)
    dt = jnp.exp(log_dt.astype(f32))[:, None]
    mag = jnp.exp(lam_re * dt)
    a_re = mag * jnp.cos(lam_im * dt)
    a_im = mag * jnp.sin(lam_im * dt)
    den = lam_re * lam_re + lam_im * lam_im
    n_re = a_re - 1.0
    z_re = (n_re * lam_re + a_im * lam_im) / den
    z_im = (a_im * lam_re - n_re * lam_im) / den
    b_re = b_re.astype(f32)
    b_im = b_im.astype(f32)
    bb_re = z_re[..., None] * b_re - z_im[..., None] * b_im
    bb_im = z_re[..., None] * b_im + z_im[..., None] * b_re
    c_re = c_re.astype(f32)
    c_im = c_im.astype(f32)

    n_chunks = seq_len // CHUNK
    u_chunks = u.reshape(bsz, n_chunks, CHUNK, N_GROUPS, SSM_GROUP).transpose(1, 0, 2, 3, 4)

    def step(carry, u_c):
        s_re, s_im = carry
        bu_re = jnp.einsum('gpc,bkgc->bkgp', bb_re, u_c)
        bu_im = jnp.einsum('gpc,bkgc->bkgp', bb_im, u_c)
        bu_re = bu_re.at[:, 0].add(a_re * s_re - a_im * s_im)
        bu_im = bu_im.at[:, 0].add(a_re * s_im + a_im * s_re)
        a_seq_re = jnp.broadcast_to(a_re, bu_re.shape)
        a_seq_im = jnp.broadcast_to(a_im, bu_im.shape)
        _, _, x_re, x_im = lax.associative_scan(
            _complex_linear_combine, (a_seq_re, a_seq_im, bu_re, bu_im), axis=1)
        y = (jnp.einsum('gcp,bkgp->bkgc', c_re, x_re)
             - jnp.einsum('gcp,bkgp->bkgc', c_im, x_im))
        return (x_re[:, -1], x_im[:, -1]), y

    init = (jnp.zeros((bsz, N_GROUPS, STATE), f32), jnp.zeros((bsz, N_GROUPS, STATE), f32))
    _, y = lax.scan(step, init, u_chunks)
    y = y.transpose(1, 0, 2, 3, 4).reshape(bsz, seq_len, D_SSM)
    y = y + d_skip.astype(f32) * u
    y = jax.nn.gelu(y).astype(h.dtype)
    y = y * jax.nn.sigmoid(y @ w_glu)
    return y @ w_out

def swiglu(h, w_gate, w_up, w_down):
    return (jax.nn.silu(h @ w_gate) * (h @ w_up)) @ w_down

def second_inputs(seed: int = 0) -> dict:
    key = jax.random.key(seed)
    ks = jax.random.split(key, 24)
    f32 = jnp.float32

    def nrm(k, shape, scale):
        return jax.random.normal(k, shape, f32) * scale

    def gain(k, shape):
        return 1.0 + 0.02 * jax.random.normal(k, shape, f32)

    x = jax.random.normal(ks[0], (BATCH, SEQ, D_MODEL), f32)
    fox_w_in = nrm(ks[1], (N_FOX, D_MODEL, 4 * D_ATT + N_HEADS), D_MODEL ** -0.5)
    fox_b_f = jax.random.uniform(ks[2], (N_FOX, N_HEADS), f32, minval=1.0, maxval=5.0)
    fox_q_gain = gain(ks[3], (N_FOX, HEAD_DIM))
    fox_k_gain = gain(ks[4], (N_FOX, HEAD_DIM))
    fox_w_out = nrm(ks[5], (N_FOX, D_ATT, D_MODEL), D_ATT ** -0.5)
    s5_w_in = nrm(ks[6], (N_S5, D_MODEL, D_SSM), D_MODEL ** -0.5)
    s5_log_dt = jax.random.uniform(ks[7], (N_S5, N_GROUPS), f32,
                                   minval=math.log(DT_MIN), maxval=math.log(DT_MAX))
    s5_lam_re = -0.5 + 0.01 * jax.random.normal(ks[8], (N_S5, N_GROUPS, STATE), f32)
    s5_lam_im = (math.pi * jnp.arange(STATE, dtype=f32)
                 + 0.01 * jax.random.normal(ks[9], (N_S5, N_GROUPS, STATE), f32))
    s5_b_re = nrm(ks[10], (N_S5, N_GROUPS, STATE, SSM_GROUP), (2 * SSM_GROUP) ** -0.5)
    s5_b_im = nrm(ks[11], (N_S5, N_GROUPS, STATE, SSM_GROUP), (2 * SSM_GROUP) ** -0.5)
    s5_c_re = nrm(ks[12], (N_S5, N_GROUPS, SSM_GROUP, STATE), (2 * STATE) ** -0.5)
    s5_c_im = nrm(ks[13], (N_S5, N_GROUPS, SSM_GROUP, STATE), (2 * STATE) ** -0.5)
    s5_d = nrm(ks[14], (N_S5, D_SSM), 1.0)
    s5_w_glu = nrm(ks[15], (N_S5, D_SSM, D_SSM), D_SSM ** -0.5)
    s5_w_out = nrm(ks[16], (N_S5, D_SSM, D_MODEL), D_SSM ** -0.5)
    mix_pre_gain = gain(ks[17], (DEPTH_2, D_MODEL))
    mix_post_gain = gain(ks[18], (DEPTH_2, D_MODEL))
    ffn_pre_gain = gain(ks[19], (DEPTH_2, D_MODEL))
    ffn_post_gain = gain(ks[20], (DEPTH_2, D_MODEL))
    ffn_w_gate = nrm(ks[21], (DEPTH_2, D_MODEL, D_FF_2), D_MODEL ** -0.5)
    ffn_w_up = nrm(ks[22], (DEPTH_2, D_MODEL, D_FF_2), D_MODEL ** -0.5)
    ffn_w_down = nrm(ks[23], (DEPTH_2, D_FF_2, D_MODEL), D_FF_2 ** -0.5)
    return {
        'x': x,
        'fox_w_in': fox_w_in, 'fox_b_f': fox_b_f, 'fox_q_gain': fox_q_gain,
        'fox_k_gain': fox_k_gain, 'fox_w_out': fox_w_out,
        's5_w_in': s5_w_in, 's5_log_dt': s5_log_dt, 's5_lam_re': s5_lam_re,
        's5_lam_im': s5_lam_im, 's5_b_re': s5_b_re, 's5_b_im': s5_b_im,
        's5_c_re': s5_c_re, 's5_c_im': s5_c_im, 's5_d': s5_d,
        's5_w_glu': s5_w_glu, 's5_w_out': s5_w_out,
        'mix_pre_gain': mix_pre_gain, 'mix_post_gain': mix_post_gain,
        'ffn_pre_gain': ffn_pre_gain, 'ffn_post_gain': ffn_post_gain,
        'ffn_w_gate': ffn_w_gate, 'ffn_w_up': ffn_w_up, 'ffn_w_down': ffn_w_down,
    }

def second_block(x, fox_w_in, fox_b_f, fox_q_gain, fox_k_gain, fox_w_out,
              s5_w_in, s5_log_dt, s5_lam_re, s5_lam_im, s5_b_re, s5_b_im,
              s5_c_re, s5_c_im, s5_d, s5_w_glu, s5_w_out,
              mix_pre_gain, mix_post_gain, ffn_pre_gain, ffn_post_gain,
              ffn_w_gate, ffn_w_up, ffn_w_down):
    for i in range(DEPTH_2):
        j = i // N_MIXERS
        h = rmsnorm(x, mix_pre_gain[i])
        if i % N_MIXERS == 0:
            m = fox_mixer(h, fox_w_in[j], fox_b_f[j], fox_q_gain[j], fox_k_gain[j], fox_w_out[j])
        else:
            m = s5_mixer(h, s5_w_in[j], s5_log_dt[j], s5_lam_re[j], s5_lam_im[j],
                         s5_b_re[j], s5_b_im[j], s5_c_re[j], s5_c_im[j], s5_d[j],
                         s5_w_glu[j], s5_w_out[j])
        x = x + rmsnorm(m, mix_post_gain[i])
        h = rmsnorm(x, ffn_pre_gain[i])
        x = x + rmsnorm(swiglu(h, ffn_w_gate[i], ffn_w_up[i], ffn_w_down[i]), ffn_post_gain[i])
    return x


def setup_inputs(seed=0):
    out = dict(first_inputs(seed))
    for name, value in second_inputs(seed + 1).items():
        if name != "x":
            out[name + "_2"] = value
    return out


def reference(
    x, c, ctx, c_ctx, ada_w, ada_b, mix_pre_g, mix_post_g, ffn_pre_g, ffn_post_g, pool_w,
    pool_scale, na_w_qkv, na_w_o, na_rpb, ffn_w_up, ffn_conv_w, ffn_conv_b, ffn_w_down,
    fox_w_in_2, fox_b_f_2, fox_q_gain_2, fox_k_gain_2, fox_w_out_2, s5_w_in_2, s5_log_dt_2,
    s5_lam_re_2, s5_lam_im_2, s5_b_re_2, s5_b_im_2, s5_c_re_2, s5_c_im_2, s5_d_2, s5_w_glu_2,
    s5_w_out_2, mix_pre_gain_2, mix_post_gain_2, ffn_pre_gain_2, ffn_post_gain_2, ffn_w_gate_2,
    ffn_w_up_2, ffn_w_down_2,
):
    x = first_block(
        x, c, ctx, c_ctx, ada_w, ada_b, mix_pre_g, mix_post_g, ffn_pre_g, ffn_post_g, pool_w,
        pool_scale, na_w_qkv, na_w_o, na_rpb, ffn_w_up, ffn_conv_w, ffn_conv_b, ffn_w_down,
    )
    return second_block(
        x, fox_w_in_2, fox_b_f_2, fox_q_gain_2, fox_k_gain_2, fox_w_out_2, s5_w_in_2,
        s5_log_dt_2, s5_lam_re_2, s5_lam_im_2, s5_b_re_2, s5_b_im_2, s5_c_re_2, s5_c_im_2,
        s5_d_2, s5_w_glu_2, s5_w_out_2, mix_pre_gain_2, mix_post_gain_2, ffn_pre_gain_2,
        ffn_post_gain_2, ffn_w_gate_2, ffn_w_up_2, ffn_w_down_2,
    )


_drawn_inputs = setup_inputs


def setup_inputs(seed=0):
    import zlib

    import numpy as np

    out = dict(_drawn_inputs(seed))
    spreads = {}
    factors = {'ffn_conv_b': 3.846,
     'fox_q_gain_2': 4.061,
     'fox_k_gain_2': 4.102,
     's5_lam_re_2': 200.0,
     'mix_post_gain_2': 2.757,
     'ffn_post_gain_2': 3.717,
     's5_log_dt_2': 37.28,
     's5_lam_im_2': 34.456,
     's5_b_re_2': 48.048,
     's5_b_im_2': 48.224,
     's5_c_re_2': 48.864,
     's5_c_im_2': 48.12}
    for name, (base, spread) in spreads.items():
        noise = np.random.default_rng([zlib.crc32(name.encode()), seed]).standard_normal(out[name].shape)
        drawn = base * np.exp(spread * noise) if base else spread * noise
        out[name] = jnp.asarray(drawn.astype(out[name].dtype))
    for name, factor in factors.items():
        out[name] = (out[name] * factor).astype(out[name].dtype)
    return out
```

```python
from contextlib import ExitStack

import numpy as np
import concourse.bass as bass
from concourse import mybir

P = 128
F32 = mybir.dt.float32
F32R = mybir.dt.float32r
BF16 = mybir.dt.bfloat16
ALU = mybir.AluOpType
ACT = mybir.ActivationFunctionType

D = 1024
T = 512
KT = D // P
FF = 2816
HT = FF // P
HH = HT // 2
EPS = 1e-6
TWO_PI = 2 * np.pi
TWO_PI_PARTS = (6.28125, 0.0019350051879882812, float(np.float32(TWO_PI - 6.28125 - 0.0019350051879882812)))
ROUND = 1.5 * 2 ** 23
PI_BELOW = 3.1415925
WINDOWS = (2, 4, 8, 16)
PAD = max(WINDOWS) // 2
HEADS = 16
HD = D // HEADS
QB = T // P
NEG = -1e30
BLK = 8
NBLK = T // BLK
CH = 16
GROUPS = D // CH
PAIRS = GROUPS // 2
STATE = 64

VECS = ["mix_pre_g", "mix_post_g", "ffn_pre_g", "ffn_post_g", "pool_scale",
        "mix_pre_0", "mix_pre_1", "mix_post_0", "mix_post_1",
        "ffn_pre_0", "ffn_pre_1", "ffn_post_0", "ffn_post_1", "s5_d"]
VCOL = {name: KT * i for i, name in enumerate(VECS)}
ADA_B = KT * len(VECS)
QK_GAIN = ADA_B + 6 * KT
NVEC = QK_GAIN + 2
SH1, SC1, G1, SH2, SC2, G2 = (KT * i for i in range(6))

S_POOL = 0
S_UP1A = S_POOL + 2
S_DN1A = S_UP1A + 2 * HH
S_UP1B = S_DN1A + KT
S_DN1B = S_UP1B + 2 * HH
S_FOX = S_DN1B + KT
S_FOXO = S_FOX + 4 * KT
S_UP2A = S_FOXO + KT
S_DN2A = S_UP2A + 2 * HH
S_UP2B = S_DN2A + KT
S_DN2B = S_UP2B + 2 * HH
S_S5I = S_DN2B + KT
S_GLU = S_S5I + KT
S_S5O = S_GLU + KT
S_UP3A = S_S5O + KT
S_DN3A = S_UP3A + 2 * HH
S_UP3B = S_DN3A + KT
S_DN3B = S_UP3B + 2 * HH
SLOTS = S_DN3B + KT
WK = KT * P
WH = HH * P


def slot_width(n):
    for s in (S_DN1A, S_DN1B, S_DN2A, S_DN2B, S_DN3A, S_DN3B):
        if s <= n < s + KT:
            return WH
    return WK


class Tally:

    def __init__(self, eng, sem):
        self.eng, self.sem, self.n, self.loop = eng, sem, 0, None

    def add(self, ins):
        ins.then_inc(self.sem, 1)
        self.n += 1

    def settle(self):
        self.eng.wait_ge(self.sem, self.n if self.loop is None else self.loop[0] * self.loop[1] + self.n)

    def enter(self, i, per, first=0):
        self.n -= first * per
        self.loop = (i, per, self.n)

    def leave(self, end):
        i, per, start = self.loop
        assert self.n - start == per, (self.n - start, per)
        self.n = start + per * end
        self.loop = None


class At:

    def __init__(self, n0, i=0, per=0):
        self.n0, self.i, self.per = n0, i, per
        self.n = n0 + i * per if per else n0
        self.s = n0 % 2
        self.turns = n0 // 2 + (i * (per // 2) if per else 0)

    def __add__(self, k):
        return At(self.n0 + k, self.i, self.per)


def steps(eng, first, count, per, body, tally=None, adds=0, lead=0):
    trips = count // per
    for i in range(lead):
        body(At(first + i * per), i)
    with eng.Fori(lead, trips - 1) as i:
        if tally:
            tally.enter(i, adds, lead)
        body(At(first, i, per), i)
        if tally:
            tally.leave(trips - 1)
    body(At(first + (trips - 1) * per), trips - 1)


def by_tile(eng, lead, first, body, tally=None, adds=0):
    for i in range(lead):
        body(i, i % 2, At(first + i))
    trips = (KT - lead) // 2
    with eng.Fori(0, trips) as t:
        if tally:
            tally.enter(t, 2 * adds)
        for p in range(2):
            body(t * 2 + (lead + p), (lead + p) % 2, At(first + lead + p, t, 2))
        if tally:
            tally.leave(trips)
    for i in range(lead + 2 * trips, KT):
        body(i, i % 2, At(first + i))


def build(nc, dram, out):
    with ExitStack() as ctx:
        top = [-(-nc.sbuf_base // 64) * 64]

        def at(name, shape, dt, offset):
            return nc.alloc_sbuf_tensor_at(name, [P] + shape, dt, offset=offset)

        def sb(name, shape, dt=F32):
            offset = top[0]
            top[0] += -(-int(np.prod(shape)) * (2 if dt == BF16 else 4) // 64) * 64
            assert top[0] <= nc.sbuf_usable_end, (name, top[0])
            return at(name, shape, dt, offset)

        def region(cols):
            offset = top[0]
            top[0] += 4 * cols
            assert top[0] <= nc.sbuf_usable_end, top[0]
            return offset

        def sem(name):
            return ctx.enter_context(nc.semaphore(name))

        x = sb("x", [KT, T])
        hh = sb("hh", [KT, T], F32R)
        hl = sb("hl", [KT, T], F32R)
        raw = sb("raw", [2, WH])
        w_hi = sb("w_hi", [2, WH], F32R)
        w_lo = sb("w_lo", [2, WH], F32R)
        vec = sb("vec", [NVEC])
        convw = sb("convw", [HT, 8])
        mods = sb("mods", [6 * KT])
        amp1 = sb("amp1", [KT])
        amp2 = sb("amp2", [KT])
        gpost1 = sb("gpost1", [KT])
        gpost2 = sb("gpost2", [KT])
        dots = sb("dots", [KT])
        eps = sb("eps", [1])
        mean = sb("mean", [P])
        r_pre = sb("r_pre", [T])
        rpost_at = top[0]
        r_post = sb("r_post", [T])
        lnr = sb("lnr", [T])
        acc_at = top[0]
        acc = sb("acc", [T])
        sq = sb("sq", [2, T])
        tmp = sb("tmp", [2, T])
        s_a = sb("s_a", [T])
        s_b = sb("s_b", [T])
        s_c = sb("s_c", [T])
        s_p = sb("s_p", [T])
        y_at = region(KT * T)
        hid_at = region(2 * HH * T)
        z_at = region(4 * 2 * WK)
        y = at("y", [KT, T], F32, y_at)
        hid_hi = at("hid_hi", [HH, T], F32R, hid_at)
        hid_lo = at("hid_lo", [HH, T], F32R, hid_at + 4 * HH * T)
        ada_w = at("ada_w", [4, 2 * D], F32, hid_at)
        csil = at("csil", [D], F32, hid_at + 4 * 8 * D)
        g2_w = at("g2_w", [3, 2 * D], F32, z_at)
        g2_csil = at("g2_csil", [D], F32, z_at + 4 * 7 * D)
        rcnt = at("rcnt", [4, T], F32, z_at)
        PW = T + 2 * PAD
        pool_s = at("pool_s", [2, PW], F32, z_at + 4 * 4 * T)
        xn = at("xn", [KT, PW], F32, z_at + 4 * (4 * T + 2 * PW))
        xm = y
        ident = sb("ident", [P])
        blk64 = sb("blk64", [P])
        ones_f = sb("ones_f", [P])
        ident_bf = sb("ident_bf", [P], BF16)
        causal = sb("causal", [P], BF16)
        ones_r = sb("ones_r", [P], F32R)
        qk_gain = sb("qk_gain", [2])
        bf_col = sb("bf_col", [1])
        nmax = sb("nmax", [QB])
        rsum = sb("rsum", [QB])
        rinv = sb("rinv", [QB])
        qk = at("qk", [4, T], F32R, y_at)
        zc = z_at
        v_hi = at("v_hi", [QB, P], F32R, zc)
        v_lo = at("v_lo", [QB, P], F32R, zc + 4 * T)
        gsig = at("gsig", [T], F32, zc + 8 * T)
        dsel = at("dsel", [2, T], F32R, zc + 12 * T)
        NP_ = P * QB * (QB + 1) // 2
        prob = at("prob", [NP_], F32, zc + 20 * T)
        pt_hi = at("pt_hi", [NP_], F32R, zc + 20 * T + 4 * NP_)
        pt_lo = at("pt_lo", [NP_], F32R, zc + 20 * T + 8 * NP_)
        assert 20 * T + 12 * NP_ <= 4 * 8 * WK
        wf_raw = at("wf_raw", [KT, P], F32, zc + 20 * T)
        wf_hi = at("wf_hi", [KT, P], F32R, zc + 20 * T + 4 * WK)
        wf_lo = at("wf_lo", [KT, P], F32R, zc + 20 * T + 8 * WK)
        tail = hid_at + 4 * KT * T
        qf = at("qf", [2, T], F32, tail)
        vt = at("vt", [T], F32, tail + 8 * T)
        tail = hid_at + 4 * (HH + KT) * T
        c_hi = at("c_hi", [T], F32R, tail)
        c_lo = at("c_lo", [T], F32R, tail + 4 * T)
        cums = at("cums", [T], F32, tail + 8 * T)
        rv_re = at("rv_re", [PAIRS, BLK], F32, acc_at)
        rv_im = at("rv_im", [PAIRS, BLK], F32, acc_at + 4 * PAIRS * BLK)
        rec = at("rec", [8, PAIRS], F32, rpost_at)
        NPW = BLK + 1
        pw_re = sb("pw_re", [PAIRS, NPW])
        pw_im = sb("pw_im", [PAIRS, NPW])
        pwn_im = sb("pwn_im", [PAIRS, NPW])
        z_re = sb("z_re", [PAIRS])
        z_im = sb("z_im", [PAIRS])
        s5s = at("s5s", [20, PAIRS], F32, z_at + 4 * (4 * T + (2 + KT) * PW))
        CW = 4 * P
        xs = at("xs", [NBLK, 2 * PAIRS], F32, z_at)
        yb = at("yb", [KT, T], F32, z_at + 4 * KT * T)
        b_raw = at("b_raw", [2, PAIRS, CH], F32, z_at + 4 * KT * T)
        hc = hid_at
        bt = at("bt", [2, PAIRS, CH], F32, hc)
        cc = at("cc", [2, PAIRS, CH], F32, hc + 4 * 2 * PAIRS * CH)
        btc = at("btc", [2, 4, CH], F32, hc + 4 * 4 * PAIRS * CH)
        hc += 4 * (4 * PAIRS * CH + 8 * CH)
        q2 = at("q2", [KT, 2, 4, P], F32, hc)
        q_tab = at("q_tab", [2, 4, P], F32, hc)
        r_tab = at("r_tab", [2, 4, P], F32, hc + 8 * CW)
        w1 = at("w1", [2, 4, P], F32, hc + 16 * CW)
        w3 = at("w3", [8, P], F32, hc + 24 * CW)
        kt = at("kt", [8, P], F32, hc + 32 * CW)
        assert hc + 4 * KT * 2 * CW <= z_at
        ub = s_a
        u_dram = nc.dram_tensor("u_scratch", (KT, P, T), F32, kind="Internal").ap()
        y_dram = nc.dram_tensor("y_scratch", (KT, P, T), F32, kind="Internal").ap()

        bank = [ctx.enter_context(nc.psum_tensor(f"bank{i}", [P, T], F32)) for i in range(8)]
        POST_BANK, PRE_BANK = 2, 3
        POOL_BANKS = [0, 2, 3, 4, 1, 5, 6, 7]

        small_in = sem("small_in")
        x_in = sem("x_in")
        x_pool = sem("x_pool")
        rcnt_in = sem("rcnt_in")
        raw_full = [sem("raw_full0"), sem("raw_full1")]
        hi_done = sem("hi_done")
        lo_done = sem("lo_done")
        slot_mm = sem("slot_mm")
        bank_free = [sem("bank_free0"), sem("bank_free1")]
        ada_full = [sem(f"ada_full{i}") for i in range(4)]
        ada_used = sem("ada_used")
        c_in = sem("c_in")
        xn_zero = sem("xn_zero")
        xm_done = sem("xm_done")
        mix_mod = sem("mix_mod")
        s5_den = sem("s5_den")
        s5_par = sem("s5_par")
        g2_in = [sem(f"g2_in{i}") for i in range(4)]
        g2_used = sem("g2_used")
        consts = sem("consts")
        csil_done = sem("csil_done")
        sq_done = sem("sq_done")
        acc_add = sem("acc_add")
        stat_x = sem("stat_x")
        stat_y = sem("stat_y")
        rpre_done = sem("rpre_done")
        rpost_done = sem("rpost_done")
        x_upd = sem("x_upd")
        hh_done = sem("hh_done")
        h_done = sem("h_done")
        conv_mid = sem("conv_mid")
        act_done = sem("act_done")
        hid_done = sem("hid_done")
        mods_done = sem("mods_done")
        dve_own = sem("dve_own")
        act_own = sem("act_own")
        stored = sem("stored")
        ident_own = sem("ident_own")
        ident_done = sem("ident_done")
        s5_small = sem("s5_small")
        s5_big = sem("s5_big")
        s5_act = sem("s5_act")
        s5_pool = sem("s5_pool")
        pool_own = sem("pool_own")
        r_done = sem("r_done")
        q_done = sem("q_done")
        rt_mm = sem("rt_mm")
        k_mm = sem("k_mm")
        w1_done = sem("w1_done")
        kt_done = sem("kt_done")
        u_out = sem("u_out")
        ub_in = sem("ub_in")
        w3_in = sem("w3_in")
        blk_mm = sem("blk_mm")
        blk_done = sem("blk_done")
        rec_done = sem("rec_done")
        q2_done = sem("q2_done")
        xc_done = sem("xc_done")
        out_mm = sem("out_mm")
        yb_done = sem("yb_done")
        y_out = [sem("y_out0"), sem("y_out1")]
        yt_in = [sem("yt_in0"), sem("yt_in1")]
        pre_gelu = sem("pre_gelu")
        gelu_done = sem("gelu_done")
        z_done = sem("z_done")
        wf_zero = sem("wf_zero")
        wf_in = sem("wf_in")
        wf_split = sem("wf_split")
        f_mm = sem("f_mm")
        f_act = sem("f_act")
        z_ready = sem("z_ready")
        sqh_done = sem("sqh_done")
        hs_mm = sem("hs_mm")
        hr_done = sem("hr_done")
        qk_done = sem("qk_done")
        vt_done = sem("vt_done")
        vt_mm = sem("vt_mm")
        vh_done = sem("vh_done")
        v_done = sem("v_done")
        g_done = sem("g_done")
        dsel_done = sem("dsel_done")
        s_mm = sem("s_mm")
        mx_done = sem("mx_done")
        exp_done = sem("exp_done")
        p_done = sem("p_done")
        t_mm = sem("t_mm")
        pth_done = sem("pth_done")
        pt_done = sem("pt_done")
        pv_mm = sem("pv_mm")
        o_done = sem("o_done")

        block = ctx.enter_context(nc.Block())

        def wait(eng, s, v):
            assert isinstance(v, int) or v.min_val > 0
            if not (isinstance(v, int) and v <= 0):
                eng.wait_ge(s, v)

        def col(name, k):
            return vec[:, VCOL[name] + k:VCOL[name] + k + 1]

        POST = [lambda k: gpost1[:, k:k + 1], lambda k: gpost2[:, k:k + 1],
                lambda k: col("mix_post_0", k), lambda k: col("ffn_post_0", k),
                lambda k: col("mix_post_1", k), lambda k: col("ffn_post_1", k)]
        PRE = [None, lambda k: col("mix_pre_0", k), lambda k: col("ffn_pre_0", k),
               lambda k: col("mix_pre_1", k), lambda k: col("ffn_pre_1", k)]
        H_SET = [1, 2, 3, 4, 6]

        S_AT = [bank[2][:, 0:P], bank[3][:, 0:2 * P], bank[2][:, P:4 * P], bank[4][:, :]]
        P_AT = [0, P, 3 * P, 6 * P]
        T_AT = [bank[5][:, :], bank[6][:, 0:3 * P], bank[3][:, 2 * P:4 * P], bank[6][:, 3 * P:4 * P]]
        PT_AT = [0, 4 * P, 8 * P, 7 * P]
        T_PARTS = [(bank[5][:, :], 0, 4 * P), (bank[6][:, :], 4 * P, 4 * P), (bank[3][:, 2 * P:4 * P], 8 * P, 2 * P)]
        PV_BANK, V_BANK = bank[7], bank[3]
        HS_BANK = [bank[2], bank[4]]

        @block.sync
        def _(sp):
            sp.dma_start(vec[:, :], dram["vec"]).then_inc(small_in, 16)
            sp.dma_start(convw[:, :, :], dram["convw"]).then_inc(small_in, 16)
            sp.dma_start(x[:, :, :], dram["x"]).then_inc(x_in, 16)
            sp.dma_start(csil[:, :], dram["c"].to_broadcast([P, D])).then_inc(c_in, 16)
            for k, name in enumerate(("s5_lam_re", "s5_lam_im")):
                sp.dma_start(s5s[:, k, :], dram[name]).then_inc(s5_small, 16)
            for h in range(2):
                sp.dma_start(s5s[STATE * h:STATE * h + STATE, 2, :],
                             dram["s5_log_dt"][h:h + 1, :].to_broadcast([STATE, PAIRS])).then_inc(s5_small, 16)
            sp.dma_start(rcnt[:, :, :], dram["rcnt"].unsqueeze(0).to_broadcast([P, 4, T])).then_inc(rcnt_in, 16)

            def load(a, src, width):
                wait(sp, hi_done, a.n - 1)
                wait(sp, lo_done, a.n - 1)
                sp.dma_start(raw[:, a.s, 0:width], src).then_inc(raw_full[a.s], 16)

            def loads(first, count, src, src0, width):
                with sp.Fori(0, count // 2) as i:
                    for s in range(2):
                        load(At(first, i, 2) + s, src[i * 2 + (src0 + s)], width)

            def load_ffn(first, up, dn, skip=0):
                loads(first + skip, 2 * HH - skip, up, skip, WK)
                loads(first + 2 * HH, KT, dn, 0, WH)
                if first == S_UP1A:
                    sp.wait_ge(g2_used, 1)
                    sp.dma_start(g2_w[:, 0, :], dram["ada_w"][4 * 5 + 3]).then_inc(g2_in[3], 16)
                loads(first + 2 * HH + KT, 2 * HH, up, 2 * HH, WK)
                loads(first + 4 * HH + KT, KT, dn, KT, WH)

            for s in range(2):
                load(At(S_POOL + s), dram["pool_w"][s], WK)
            for b in range(4):
                sp.dma_start(ada_w[:, b, :], dram["ada_w"][b]).then_inc(ada_full[b], 16)
            with sp.Fori(0, 4) as i:
                for b in range(4):
                    sp.wait_ge(ada_used, i * 4 + b + 1)
                    sp.dma_start(ada_w[:, b, :], dram["ada_w"][i * 4 + b + 4]).then_inc(ada_full[b], 16)
            for s in range(2):
                load(At(S_UP1A + s), dram["up1"][s], WK)
            sp.wait_ge(h_done, KT)
            sp.wait_ge(s5_par, 3)
            sp.dma_start(g2_csil[:, :], dram["c"].to_broadcast([P, D])).then_inc(c_in, 16)
            for b in range(3):
                sp.dma_start(g2_w[:, b, :], dram["ada_w"][4 * 5 + b]).then_inc(g2_in[b], 16)
            load_ffn(S_UP1A, dram["up1"], dram["dn1"], skip=2)
            for s in range(2):
                load(At(S_FOX + s), dram["fox_in"][s], WK)
            sp.wait_ge(wf_zero, 1)
            sp.dma_start(wf_raw[:, :, 0:HEADS], dram["fox_f"]).then_inc(wf_in, 16)
            sp.dma_start(bf_col[0:HEADS, :], dram["fox_bf"]).then_inc(wf_in, 16)
            loads(S_FOX + 2, 4 * KT - 2, dram["fox_in"], 2, WK)
            loads(S_FOXO, KT, dram["fox_out"], 0, WK)
            load_ffn(S_UP2A, dram["up2"], dram["dn2"])
            for s in range(2):
                load(At(S_S5I + s), dram["s5_w"][s], WK)
            sp.wait_ge(slot_mm, S_S5I)
            sp.dma_start(b_raw[:, :, :, :], dram["s5_b"]).then_inc(s5_big, 16)
            sp.dma_start(cc[:, :, :, :], dram["s5_c"]).then_inc(s5_big, 16)

            def s5_in_step(i, p, a):
                load(a + 2, dram["s5_w"][i + 2], WK)
                sp.wait_ge(bank_free[p], a.turns + 1)
                sp.dma_start(u_dram[i], y[:, i, :]).then_inc(u_out, 16)
                sp.wait_ge(u_out, (i + 1) * 16)
                wait(sp, blk_mm, i)
                src = u_dram[i].rearrange("(g c) (s j) -> s c g j", c=CH, s=BLK)
                for t in range(BLK):
                    sp.dma_start(ub[CH * t:CH * t + CH, :].rearrange("p (g j) -> p g j", g=8), src[t])\
                      .then_inc(ub_in, 16)
                sp.wait_ge(kt_done, (i + 1) * 2)
                for t in range(BLK):
                    sp.dma_start(w3[CH * t:CH * t + CH, :, CH * t:P], kt[0:CH, :, 0:P - CH * t]).then_inc(w3_in, 16)
            by_tile(sp, 1, S_S5I, s5_in_step)

            def y_back(i, p):
                sp.wait_ge(y_out[p], (i - p) * 8 + 16)
                if not isinstance(i, int) or i >= 2:
                    sp.wait_ge(pre_gelu, i - 1)
                src = y_dram[i].rearrange("(s c) (g j) -> g c s j", c=CH, g=8)
                for g in range(8):
                    sp.dma_start(tmp[CH * g:CH * g + CH, p, :].rearrange("p (s j) -> p s j", s=BLK), src[g])\
                      .then_inc(yt_in[p], 16)

            def s5_out_step(i, p, a):
                sp.wait_ge(yb_done, i + 1)
                sp.dma_start(y_dram[i], yb[:, i, :]).then_inc(y_out[p], 16)
                if not isinstance(i, int) or i >= 1:
                    y_back(i - 1, 1 - p)
            by_tile(sp, 4, 0, s5_out_step)
            y_back(KT - 1, (KT - 1) % 2)
            loads(S_GLU + 2, 2 * KT - 2, dram["s5_w"], KT + 2, WK)
            load_ffn(S_UP3A, dram["up3"], dram["dn3"])
            for k in range(KT):
                sp.wait_ge(x_upd, 5 * KT + k + 1)
                sp.dma_start(out[:, k, :], x[:, k, :]).then_inc(stored, 16)
            sp.wait_ge(stored, 16 * KT)

        @block.scalar
        def _(act):
            own = Tally(act, act_own)

            def hi(a):
                if a.n0 >= SLOTS:
                    return
                width = slot_width(a.n0)
                act.wait_ge(raw_full[a.s], (a.turns + 1) * 16)
                wait(act, slot_mm, a.n - 1)
                act.activation(w_hi[:, a.s, 0:width], raw[:, a.s, 0:width], ACT.Copy).then_inc(hi_done, 1)

            def rsqrt(dst, b, done):
                own.add(act.activation(lnr[:, :], bank[b][:, :], ACT.Ln, bias=eps[:, 0:1]))
                own.settle()
                act.activation(dst[:, :], lnr[:, :], ACT.Exp, scale=-0.5).then_inc(done, 1)

            def squares_x(q, k):
                wait(act, stat_x, KT * q + k - 1 if k >= 2 else 0)
                act.activation(sq[:, k % 2, :], x[:, k, :], ACT.Square).then_inc(sq_done, 1)

            def boundary(q):
                act.wait_ge(stat_y, q + 1)
                rsqrt(r_post, POST_BANK, rpost_done)
                if q == len(POST) - 1:
                    return
                for k in range(KT):
                    act.wait_ge(x_upd, KT * q + k + 1)
                    if PRE[q]:
                        act.activation(hh[:, k, :], x[:, k, :], ACT.Copy, scale=PRE[q](k)).then_inc(hh_done, 1)
                    squares_x(q + 1, k)
                act.wait_ge(stat_x, KT * (q + 2))
                rsqrt(r_pre, PRE_BANK, rpre_done)

            def y_square(q, a, m, k2):
                act.wait_ge(bank_free[a.s], a.turns + 1)
                act.wait_ge(acc_add, m + KT * q - 1) if q else None
                act.activation(sq[:, k2, :], y[:, m, :], ACT.Square).then_inc(sq_done, 1)

            def down(q, first):
                def first_half(a, j):
                    for s in range(2):
                        hi(a + (s + 2))

                def second_half(a, j):
                    for s in range(2):
                        hi(a + (s + 2))
                        y_square(q, a + s, j * 2 + s, s)
                return first_half, second_half

            def conv_up(half, base):
                def body(a, j):
                    i = j + half * HH
                    for s in range(2):
                        hi(a + (s + 2))
                        act.wait_ge(slot_mm, (a + s).n + 1)
                        wait(act, hid_done, base + j)
                        act.activation([s_a, s_c][s][:, :], bank[s][:, :], ACT.Identity,
                                       scale=convw[:, i, 4 * s + 1:4 * s + 2],
                                       bias=convw[:, i, 4 * s + 3:4 * s + 4]).then_inc(conv_mid, 1)
                        if s == 0:
                            act.wait_ge(bank_free[0], (a + 0).turns + 1)
                            act.activation(s_b[:, :], s_a[:, :], ACT.Gelu_apprx_tanh).then_inc(act_done, 1)
                return body

            def silu_up(half, base):
                def body(a, j):
                    hi(a + 2)
                    act.wait_ge(bank_free[0], a.turns + 1)
                    act.activation(s_b[:, :], s_a[:, :], ACT.Silu).then_inc(act_done, 1)
                    hi(a + 3)
                return body

            def ffn(q, first, up, base):
                lo_half, hi_half = down(q, first)
                steps(act, first, 2 * HH, 2, up(0, base), lead=1)
                if q == 1:
                    act.wait_ge(c_in, 32)
                    act.activation(g2_csil[:, :], g2_csil[:, :], ACT.Silu).then_inc(csil_done, 1)
                steps(act, first + 2 * HH, KT, 2, lo_half)
                steps(act, first + 2 * HH + KT, 2 * HH, 2, up(1, base + HH))
                steps(act, first + 4 * HH + KT, KT, 2, hi_half)

            def attend(jj, head, exp=False, pt=False):
                hd = jj * 2 + head
                if exp:
                    act.wait_ge(mx_done, hd + 1)
                    for qb in range(QB):
                        w = P * (qb + 1)
                        e = act.activation(prob[:, P_AT[qb]:P_AT[qb] + w], S_AT[qb], ACT.Exp,
                                           bias=nmax[:, qb:qb + 1], accum_out=rsum[:, qb:qb + 1])
                    e.then_inc(exp_done, 1)
                if pt:
                    act.wait_ge(t_mm, hd + 1)
                    wait(act, pv_mm, hd)
                    for b, c, w in T_PARTS:
                        act.activation(pt_hi[:, c:c + w], b, ACT.Copy).then_inc(pth_done, 1)

            def fox_step(a, j, jj, slots, att):
                if slots:
                    hi(a + 2)
                    act.wait_ge(bank_free[0], a.turns + 1)
                    act.activation(sq[:, 0, :], qf[:, 0, :], ACT.Square).then_inc(sqh_done, 1)
                if att:
                    attend(jj, 0, exp=True)
                if slots:
                    hi(a + 3)
                    act.wait_ge(bank_free[1], (a + 1).turns + 1)
                    act.activation(sq[:, 1, :], qf[:, 1, :], ACT.Square).then_inc(sqh_done, 1)
                if att:
                    attend(jj, 0, pt=True)
                if slots:
                    hi(a + 4)
                if att:
                    attend(jj, 1, exp=True)
                if slots:
                    hi(a + 5)
                if att:
                    attend(jj, 1, pt=True)
                if slots:
                    for t, dst in enumerate((s_b, s_c)):
                        act.wait_ge(hs_mm, j * 2 + (t + 1))
                        if t:
                            act.wait_ge(hr_done, j * 2 + 1)
                        own.add(act.activation(lnr[:, :], HS_BANK[t][:, :], ACT.Ln, bias=eps[:, 0:1]))
                        own.settle()
                        act.activation(dst[:, :], lnr[:, :], ACT.Exp, scale=-0.5).then_inc(hr_done, 1)
                    act.wait_ge(vt_mm, j + 1)
                    if att:
                        act.wait_ge(pv_mm, jj * 2 + 2)
                    act.activation(v_hi[:, :, :].rearrange("p a b -> p (a b)"), V_BANK[:, :], ACT.Copy).then_inc(vh_done, 1)
                    act.wait_ge(bank_free[1], (a + 3).turns + 1)
                    if att:
                        act.wait_ge(o_done, jj * 2 + 2)
                    act.activation(gsig[:, :], s_a[:, :], ACT.Sigmoid).then_inc(g_done, 1)

            def fox():
                act.wait_ge(wf_in, 32)
                act.activation(wf_hi[:, :, :], wf_raw[:, :, :], ACT.Copy).then_inc(wf_split, 1)
                fox_step(At(S_FOX), 0, None, True, False)
                act.wait_ge(z_ready, 1)
                lz = cums[0:HEADS, :]
                own.add(act.activation(lz, s_p[0:HEADS, :], ACT.Abs))
                own.settle()
                own.add(act.activation(lz, lz, ACT.Exp, scale=-1.0))
                own.settle()
                act.activation(lz, lz, ACT.Ln, bias=1.0).then_inc(f_act, 1)
                fox_step(At(S_FOX + 4), 1, 0, True, True)
                with act.Fori(1, KT - 1) as i:
                    own.enter(i, 2, 1)
                    fox_step(At(S_FOX + 4, i, 4), i + 1, i, True, True)
                    own.leave(KT - 1)
                fox_step(None, None, KT - 1, False, True)
                steps(act, S_FOXO, KT, 2, down(2, S_FOXO)[1])

            def s5_small_functions():
                act.wait_ge(s5_small, 64)
                act.activation(s5s[:, 3, :], s5s[:, 2, :], ACT.Exp).then_inc(s5_act, 1)
                act.wait_ge(s5_par, 1)
                act.activation(s5s[:, 6, :], s5s[:, 4, :], ACT.Exp).then_inc(s5_act, 1)
                act.wait_ge(s5_par, 2)
                act.activation(s5s[:, 9, :], s5s[:, 7, :], ACT.Sin).then_inc(s5_act, 1)
                act.activation(s5s[:, 10, :], s5s[:, 8, :], ACT.Sin).then_inc(s5_act, 1)

            def s5():
                def in_step(i, p, a):
                    hi(a + 2)
                    act.wait_ge(rt_mm, i + 1)
                    for t in range(2):
                        act.activation(w1[:, t, :, :].rearrange("p a b -> p (a b)"), bank[2 + t][:, :], ACT.Copy)\
                           .then_inc(w1_done, 1)
                    act.wait_ge(k_mm, i + 1)
                    wait(act, w3_in, i * (16 * BLK))
                    for t in range(2):
                        act.activation(kt[0:CH, 4 * t:4 * t + 4, :].rearrange("p a b -> p (a b)"),
                                       bank[4 + t][0:CH, :], ACT.Copy).then_inc(kt_done, 1)
                by_tile(act, 1, S_S5I, in_step)

                def out_step(i, p, a):
                    act.wait_ge(rec_done, 1)
                    if not isinstance(i, int) or i >= 2:
                        act.wait_ge(out_mm, i - 1)
                    src = xs[:, :, :].rearrange("p j (t i r) -> p t i r j", t=2, r=4)
                    for t in range(2):
                        act.activation(sq[:, p, 4 * NBLK * t:4 * NBLK * (t + 1)].rearrange("p (r j) -> p r j", r=4),
                                       src[:, t, i, :, :], ACT.Copy).then_inc(xc_done, 1)
                    if not isinstance(i, int) or i >= 2:
                        gelu(i - 2, p)

                def gelu(i, p):
                    act.wait_ge(pre_gelu, i + 1)
                    act.activation(y[:, i, :], [s_p, lnr][p][:, :], ACT.Gelu_apprx_tanh).then_inc(gelu_done, 1)
                by_tile(act, 2, 0, out_step)
                gelu(KT - 2, 0)
                gelu(KT - 1, 1)

                def glu(a, j):
                    for s in range(2):
                        hi(a + (s + 2))
                        act.wait_ge(slot_mm, (a + s).n + 1)
                        wait(act, z_done, j * 2)
                        act.activation([s_b, s_c][s][:, :], bank[s][:, :], ACT.Sigmoid).then_inc(bank_free[s], 1)
                steps(act, S_GLU, KT, 2, glu, lead=1)
                steps(act, S_S5O, KT, 2, down(4, S_S5O)[1])

            act.wait_ge(x_in, 16)
            for k in range(KT):
                squares_x(0, k)
            act.wait_ge(c_in, 16)
            act.activation(csil[:, :], csil[:, :], ACT.Silu).then_inc(csil_done, 1)
            act.wait_ge(consts, 1)
            act.wait_ge(stat_x, KT)
            rsqrt(r_pre, PRE_BANK, rpre_done)
            hi(At(0))
            hi(At(1))
            act.wait_ge(mods_done, 1)
            for k in range(KT):
                act.wait_ge(xm_done, k + 1)
                wait(act, h_done, k - 1)
                for src, dst in ((xm[:, k, :], tmp), (xn[:, k, PAD:PAD + T], sq)):
                    act.activation(dst[:, k % 2, :], src, ACT.Identity, scale=amp1[:, k:k + 1],
                                   bias=mods[:, SH1 + k:SH1 + k + 1]).then_inc(mix_mod, 1)
            s5_small_functions()
            for m in range(KT):
                if m % 4 == 0:
                    hi(At(S_POOL + m // 4 + 2))
                act.wait_ge(x_pool, m + 1)
                wait(act, acc_add, m - 1)
                act.activation(sq[:, m % 2, :], y[:, m, :], ACT.Square).then_inc(sq_done, 1)
            boundary(0)
            ffn(1, S_UP1A, conv_up, 0)
            boundary(1)
            fox()
            boundary(2)
            ffn(3, S_UP2A, silu_up, 2 * HH)
            boundary(3)
            s5()
            boundary(4)
            ffn(5, S_UP3A, silu_up, 4 * HH)
            boundary(5)

        @block.vector
        def _(dve):
            own = Tally(dve, dve_own)

            def lo(a):
                if a.n0 >= SLOTS:
                    return
                width = slot_width(a.n0)
                dve.wait_ge(hi_done, a.n + 1)
                dve.tensor_tensor(w_lo[:, a.s, 0:width], raw[:, a.s, 0:width],
                                  w_hi[:, a.s, 0:width].bitcast(F32), ALU.subtract).then_inc(lo_done, 1)

            def split(src, dst_hi, dst_lo, done):
                own.settle()
                own.add(dve.tensor_copy(dst_hi, src))
                own.settle()
                dve.tensor_tensor(dst_lo, src, dst_hi.bitcast(F32), ALU.subtract).then_inc(done, 1)

            def add_square(q, m, k2):
                dve.wait_ge(sq_done, m + (KT + 2 * KT * q + 1))
                own.settle()
                own.add(dve.tensor_tensor(acc[:, :], acc[:, :], sq[:, k2, :], ALU.add))
                own.settle()
                dve.sem_inc(acc_add, 1)

            def boundary(q):
                dve.wait_ge(rpost_done, q + 1)
                for k in range(KT + 1):
                    if k < KT:
                        own.add(dve.scalar_tensor_tensor(tmp[:, k % 2, :], y[:, k, :], POST[q](k),
                                                         r_post[:, :], ALU.mult, ALU.mult))
                        own.settle()
                        dve.tensor_tensor(x[:, k, :], x[:, k, :], tmp[:, k % 2, :], ALU.add).then_inc(x_upd, 1)
                    if k and q < len(PRE) and PRE[q]:
                        dve.wait_ge(hh_done, hh_before[q] + k)
                        dve.scalar_tensor_tensor(hl[:, k - 1, :], x[:, k - 1, :], PRE[q](k - 1),
                                                 hh[:, k - 1, :].bitcast(F32), ALU.mult,
                                                 ALU.subtract).then_inc(h_done, 1)
                if q == 0:
                    dve.wait_ge(rpre_done, 2)
                    for k in range(KT):
                        own.add(dve.scalar_tensor_tensor(tmp[:, k % 2, :], x[:, k, :], amp2[:, k:k + 1],
                                                         r_pre[:, :], ALU.mult, ALU.mult))
                        own.settle()
                        own.add(dve.tensor_scalar(s_a[:, :], tmp[:, k % 2, :], mods[:, SH2 + k:SH2 + k + 1], None,
                                                  ALU.add))
                        split(s_a[:, :], hh[:, k, :], hl[:, k, :], h_done)

            def down(q):
                def first_half(a, j):
                    for s in range(2):
                        lo(a + (s + 2))
                        dve.wait_ge(slot_mm, (a + s).n + 1)
                        dve.tensor_copy(y[:, j * 2 + s, :], bank[s][:, :]).then_inc(bank_free[s], 1)

                def second_half(a, j):
                    for s in range(2):
                        lo(a + (s + 2))
                        dve.wait_ge(slot_mm, (a + s).n + 1)
                        m = j * 2 + s
                        dve.tensor_tensor(y[:, m, :], y[:, m, :], bank[s][:, :], ALU.add).then_inc(bank_free[s], 1)
                        add_square(q, m, s)
                return first_half, second_half

            def conv_up(half, base):
                def body(a, j):
                    i = j + half * HH
                    for s in range(2):
                        lo(a + (s + 2))
                        c = [s_a, s_c][s]
                        b = bank[s]
                        dve.wait_ge(conv_mid, (j + base) * 2 + s + 1)
                        own.add(dve.scalar_tensor_tensor(c[:, 1:T], b[:, 0:T - 1], convw[:, i, 4 * s:4 * s + 1],
                                                         c[:, 1:T], ALU.mult, ALU.add))
                        own.settle()
                        dve.scalar_tensor_tensor(c[:, 0:T - 1], b[:, 1:T], convw[:, i, 4 * s + 2:4 * s + 3],
                                                 c[:, 0:T - 1], ALU.mult, ALU.add).then_inc(bank_free[s], 1)
                    dve.wait_ge(act_done, j + base + 1)
                    dve.wait_ge(bank_free[1], (a + 1).turns + 1)
                    own.add(dve.tensor_tensor(s_p[:, :], s_b[:, :], s_c[:, :], ALU.mult))
                    split(s_p[:, :], hid_hi[:, j, :], hid_lo[:, j, :], hid_done)
                return body, 4

            def silu_up(half, base):
                def body(a, j):
                    lo(a + 2)
                    dve.wait_ge(slot_mm, a.n + 1)
                    dve.tensor_tensor(s_a[:, :], bank[0][:, :], r_pre[:, :], ALU.mult).then_inc(bank_free[0], 1)
                    lo(a + 3)
                    dve.wait_ge(act_done, j + base + 1)
                    own.add(dve.tensor_tensor(s_c[:, :], s_b[:, :], r_pre[:, :], ALU.mult))
                    own.settle()
                    dve.wait_ge(slot_mm, a.n + 2)
                    dve.tensor_tensor(s_p[:, :], s_c[:, :], bank[1][:, :], ALU.mult).then_inc(bank_free[1], 1)
                    dve.wait_ge(bank_free[1], (a + 1).turns + 1)
                    split(s_p[:, :], hid_hi[:, j, :], hid_lo[:, j, :], hid_done)
                return body, 2

            def ffn(q, first, up, base):
                lo_half, hi_half = down(q)
                dve.wait_ge(rpre_done, q + 1)
                body, adds = up(0, base)
                steps(dve, first, 2 * HH, 2, body, own, adds)
                if q == 1:
                    dve.wait_ge(csil_done, 2)
                    for b in range(3):
                        dve.wait_ge(g2_in[b], 16)
                        two_dots(g2_w[:, b, :], g2_csil, b, g2_used)
                steps(dve, first + 2 * HH, KT, 2, lo_half)
                if q == 1:
                    dve.wait_ge(g2_in[3], 16)
                    two_dots(g2_w[:, 0, :], g2_csil, 3, g2_used)
                body, adds = up(1, base + HH)
                steps(dve, first + 2 * HH + KT, 2 * HH, 2, body, own, adds)
                own.add(dve.memset(acc[:, :], 0.0))
                steps(dve, first + 4 * HH + KT, KT, 2, hi_half, own, 2)

            def mixer_out(q):
                def body(a, j):
                    for s in range(2):
                        lo(a + (s + 2))
                        dve.wait_ge(slot_mm, (a + s).n + 1)
                        m = j * 2 + s
                        dve.tensor_copy(y[:, m, :], bank[s][:, :]).then_inc(bank_free[s], 1)
                        add_square(q, m, s)
                return body

            def select_c(jj, head):
                hd = jj * 2 + head
                wait(dve, s_mm, hd)
                for t, src in enumerate((c_hi, c_lo)):
                    dve.tensor_scalar(dsel[0:HEADS, t, :], src[0:HEADS, :].bitcast(F32), head_col(jj, head),
                                      None, ALU.mult).then_inc(dsel_done, 1)

            def head_col(jj, head):
                return ident[0:HEADS, 0:HEADS].rearrange("p (j h) -> p j h", h=2)[:, jj, head:head + 1]

            def softmax(jj, head):
                hd = jj * 2 + head
                dve.wait_ge(s_mm, hd + 1)
                for qb in range(QB):
                    own.add(dve.tensor_reduce(rinv[:, qb:qb + 1], S_AT[qb], mybir.AxisListType.X, ALU.max))
                own.settle()
                dve.tensor_scalar(nmax[:, :], rinv[:, :], -1.0, None, ALU.mult).then_inc(mx_done, 1)
                dve.wait_ge(exp_done, hd + 1)
                own.add(dve.reciprocal(rinv[:, :], rsum[:, :]))
                own.settle()
                for qb in range(QB):
                    pr = prob[:, P_AT[qb]:P_AT[qb] + P * (qb + 1)]
                    p = dve.tensor_scalar(pr, pr, rinv[:, qb:qb + 1], None, ALU.mult)
                p.then_inc(p_done, 1)

            def pt_split(jj, head):
                hd = jj * 2 + head
                for t, (b, c, w) in enumerate(T_PARTS):
                    dve.wait_ge(pth_done, hd * 3 + (t + 1))
                    dve.tensor_tensor(pt_lo[:, c:c + w], b, pt_hi[:, c:c + w].bitcast(F32), ALU.subtract)\
                       .then_inc(pt_done, 1)

            def head_out(jj, head):
                r = slice(HD * head, HD * head + HD)
                dve.wait_ge(pv_mm, jj * 2 + (head + 1))
                dve.wait_ge(g_done, jj + 1)
                own.add(dve.tensor_tensor(s_p[r, :], PV_BANK[r, :], gsig[r, :], ALU.mult))
                split(s_p[r, :], hid_hi[r, jj, :], hid_lo[r, jj, :], o_done)

            def fox_step(a, j, jj, slots, att):
                if att:
                    select_c(jj, 0)
                if slots:
                    lo(a + 2)
                    dve.wait_ge(slot_mm, a.n + 1)
                    dve.tensor_tensor(qf[:, 0, :], bank[0][:, :], r_pre[:, :], ALU.mult).then_inc(bank_free[0], 1)
                if att:
                    softmax(jj, 0)
                    select_c(jj, 1)
                if slots:
                    lo(a + 3)
                    dve.wait_ge(slot_mm, a.n + 2)
                    dve.tensor_tensor(qf[:, 1, :], bank[1][:, :], r_pre[:, :], ALU.mult).then_inc(bank_free[1], 1)
                if att:
                    pt_split(jj, 0)
                if slots:
                    lo(a + 4)
                    dve.wait_ge(slot_mm, a.n + 3)
                    own.add(dve.tensor_tensor(vt[:, :], bank[0][:, :], r_pre[:, :], ALU.mult))
                    own.settle()
                    dve.sem_inc(bank_free[0], 1)
                    dve.sem_inc(vt_done, 1)
                if att:
                    head_out(jj, 0)
                    softmax(jj, 1)
                if slots:
                    lo(a + 5)
                    dve.wait_ge(slot_mm, a.n + 4)
                    if att:
                        dve.wait_ge(g_done, jj + 1)
                    dve.tensor_tensor(s_a[:, :], bank[1][:, :], r_pre[:, :], ALU.mult).then_inc(bank_free[1], 1)
                if att:
                    pt_split(jj, 1)
                if slots:
                    for t, hr in enumerate((s_b, s_c)):
                        dve.wait_ge(hr_done, j * 2 + (t + 1))
                        if att:
                            dve.wait_ge(s_mm, jj * 2 + 2)
                        own.add(dve.scalar_tensor_tensor(tmp[:, t, :], qf[:, t, :], qk_gain[:, t:t + 1], hr[:, :],
                                                         ALU.mult, ALU.mult))
                        split(tmp[:, t, :], qk[:, 2 * t, :], qk[:, 2 * t + 1, :], qk_done)
                if att:
                    head_out(jj, 1)
                if slots:
                    dve.wait_ge(vh_done, j + 1)
                    flat = "p a b -> p (a b)"
                    dve.tensor_tensor(v_lo[:, :, :].rearrange(flat), V_BANK[:, :],
                                      v_hi[:, :, :].rearrange(flat).bitcast(F32), ALU.subtract).then_inc(v_done, 1)

            def fox():
                own.add(dve.tensor_scalar(qk_gain[:, 0:1], vec[:, QK_GAIN:QK_GAIN + 1], HD ** -0.5, None, ALU.mult))
                own.add(dve.tensor_copy(qk_gain[:, 1:2], vec[:, QK_GAIN + 1:QK_GAIN + 2]))
                own.add(dve.memset(dsel[:, :, :].bitcast(mybir.dt.uint32), 0))
                dve.wait_ge(wf_split, 1)
                dve.tensor_tensor(wf_lo[:, :, :], wf_raw[:, :, :], wf_hi[:, :, :].bitcast(F32), ALU.subtract)\
                   .then_inc(wf_split, 1)
                dve.wait_ge(rpre_done, 3)
                fox_step(At(S_FOX), 0, None, True, False)
                dve.wait_ge(f_mm, 1)
                z, lf, one = s_p[0:HEADS, :], vt[0:HEADS, :], tmp[0:HEADS, 0, :]
                own.add(dve.tensor_tensor(lf, bank[5][0:HEADS, :], r_pre[0:HEADS, :], ALU.mult))
                own.settle()
                own.add(dve.tensor_scalar(z, lf, bf_col[0:HEADS, 0:1], None, ALU.add))
                own.settle()
                dve.sem_inc(z_ready, 1)
                own.add(dve.tensor_scalar(lf, z, 0.0, None, ALU.min))
                own.add(dve.memset(one, 1.0))
                own.settle()
                dve.wait_ge(f_act, 1)
                own.add(dve.tensor_tensor(lf, lf, cums[0:HEADS, :], ALU.subtract))
                own.settle()
                own.add(dve.tensor_tensor_scan(cums[0:HEADS, :], one, lf, 0.0, ALU.mult, ALU.add))
                own.settle()
                own.add(dve.tensor_scalar(z, cums[0:HEADS, :], -1.0, None, ALU.mult))
                own.settle()
                own.add(dve.tensor_copy(c_hi[0:HEADS, :], z))
                own.settle()
                own.add(dve.tensor_tensor(c_lo[0:HEADS, :], z, c_hi[0:HEADS, :].bitcast(F32), ALU.subtract))
                own.settle()
                fox_step(At(S_FOX + 4), 1, 0, True, True)
                with dve.Fori(1, KT - 1) as i:
                    own.enter(i, FOX_ADDS, 1)
                    fox_step(At(S_FOX + 4, i, 4), i + 1, i, True, True)
                    own.leave(KT - 1)
                fox_step(None, None, KT - 1, False, True)
                own.add(dve.memset(acc[:, :], 0.0))
                steps(dve, S_FOXO, KT, 2, mixer_out(2), own, 2)

            def tt(out_, a, b, op):
                own.add(dve.tensor_tensor(out_, a, b, op))
                own.settle()

            def ts(out_, a, s1, s2, op0, op1=None):
                own.add(dve.tensor_scalar(out_, a, s1, s2, op0) if op1 is None else
                        dve.tensor_scalar(out_, a, s1, s2, op0, op1))
                own.settle()

            def two_dots(w, c, b, used):
                for t in range(2):
                    wt = w[:, t * D:(t + 1) * D]
                    dot = dve.tensor_tensor_reduce(wt, wt, c[:, :], 1.0, 0.0, ALU.mult, ALU.add,
                                                   accum_out=dots[:, 2 * b + t:2 * b + t + 1])
                dot.then_inc(used, 1)

            def add_bias(i):
                six = "p (i k) -> p i k"
                own.add(dve.tensor_tensor(mods[:, :].rearrange(six, k=KT)[:, i, :], dots[:, :],
                                          vec[:, ADA_B:ADA_B + 6 * KT].rearrange(six, k=KT)[:, i, :], ALU.add))
                own.settle()

            def modulation(i):
                for b in range(4):
                    dve.wait_ge(ada_full[b], (i + 1) * 16)
                    two_dots(ada_w[:, b, :], csil, b, ada_used)
                dve.wait_ge(ada_used, (i + 1) * 4)
                add_bias(i)

            def scaled(dst, first, name, plus):
                own.add(dve.scalar_tensor_tensor(dst[:, :], mods[:, first:first + KT], plus,
                                                 vec[:, VCOL[name]:VCOL[name] + KT], ALU.add, ALU.mult))

            def s5():
                by_block = "p (j s) -> p s j"
                dve.wait_ge(rpre_done, 5)
                dve.wait_ge(s5_par, 3)

                def blocks_out(i):
                    dve.wait_ge(blk_mm, i + 1)
                    dst = xs[:, :, :].rearrange("p j (t i r) -> p t i r j", t=2, r=4)
                    for t in range(2):
                        dve.tensor_copy(dst[:, t, i, :, :],
                                        bank[6][:, 4 * NBLK * t:4 * NBLK * (t + 1)].rearrange("p (r j) -> p r j", r=4))\
                           .then_inc(blk_done, 1)
                    dve.tensor_copy(yb[:, i, :], bank[7][:, :]).then_inc(blk_done, 1)

                def in_step(i, p, a):
                    lo(a + 2)
                    dve.wait_ge(slot_mm, a.n + 1)
                    dve.tensor_tensor(y[:, i, :].rearrange("p (s j) -> p s j", s=BLK),
                                      bank[p][:, :].rearrange(by_block, s=BLK),
                                      r_pre[:, :].rearrange(by_block, s=BLK), ALU.mult).then_inc(bank_free[p], 1)
                    if not isinstance(i, int) or i:
                        blocks_out(i - 1)
                by_tile(dve, 1, S_S5I, in_step)
                blocks_out(KT - 1)

                a8r = rec[:, 0:2, :]
                a8i = rec[:, 2:4, :]
                for h in range(2):
                    own.add(dve.tensor_copy(rec[:, h, :], pw_re[:, :, BLK]))
                own.add(dve.tensor_copy(rec[:, 2, :], pwn_im[:, :, BLK]))
                own.add(dve.tensor_copy(rec[:, 3, :], pw_im[:, :, BLK]))
                dve.wait_ge(blk_done, 3 * KT)
                states = xs[:, :, :].rearrange("p j (t r) -> p j t r", t=2)
                UN = 9
                with dve.Fori(0, (NBLK - 1) // UN) as jj:
                    own.enter(jj, 5 * UN)
                    for t in range(UN):
                        before, now = states[:, jj * UN + t, :, :], states[:, jj * UN + (t + 1), :, :]
                        own.settle()
                        own.add(dve.tensor_tensor(rec[:, 4:6, :], a8r, before, ALU.mult))
                        for h in range(2):
                            own.add(dve.tensor_tensor(rec[:, 6 + h, :], rec[:, 2 + h, :], before[:, 1 - h, :],
                                                      ALU.mult))
                        own.settle()
                        own.add(dve.tensor_tensor(rec[:, 6:8, :], rec[:, 6:8, :], rec[:, 4:6, :], ALU.add))
                        own.settle()
                        own.add(dve.tensor_tensor(now, now, rec[:, 6:8, :], ALU.add))
                    own.leave((NBLK - 1) // UN)
                own.settle()
                dve.sem_inc(rec_done, 1)

                def pre(i, p):
                    dve.wait_ge(yt_in[p], (i - p) * 64 + 128)
                    if not isinstance(i, int) or i >= 2:
                        dve.wait_ge(gelu_done, i - 1)
                    dve.scalar_tensor_tensor([s_p, lnr][p][:, :], y[:, i, :], s5_d_col(i), tmp[:, p, :],
                                             ALU.mult, ALU.add).then_inc(pre_gelu, 1)

                def s5_d_col(i):
                    return vec[:, VCOL["s5_d"]:VCOL["s5_d"] + KT].rearrange("p (k o) -> p k o", o=1)[:, i, :]

                def post(i):
                    dve.wait_ge(gelu_done, i + 1)
                    own.add(dve.tensor_copy(hh[:, i, :], y[:, i, :]))
                    own.settle()
                    dve.tensor_tensor(hl[:, i, :], y[:, i, :], hh[:, i, :].bitcast(F32), ALU.subtract)\
                       .then_inc(h_done, 1)

                def out_step(i, p, a):
                    dve.wait_ge(out_mm, i + 1)
                    for h in range(2):
                        dst = yb[:, i, :].rearrange("p (g h j) -> p h g j", h=2, j=NBLK)[:, h, :, 1:NBLK]
                        add = dve.tensor_tensor(dst, dst, bank[4 + 2 * p + h][:, 0:4 * NBLK].rearrange(
                            "p (g j) -> p g j", g=4)[:, :, 0:NBLK - 1], ALU.add)
                    add.then_inc(yb_done, 1)
                    if not isinstance(i, int) or i >= 2:
                        pre(i - 2, p)
                    if not isinstance(i, int) or i >= 3:
                        post(i - 3)
                by_tile(dve, 4, 0, out_step, own, 1)
                for i in range(KT - 2, KT):
                    pre(i, i % 2)
                    post(i - 1)
                post(KT - 1)

                def glu(a, j):
                    for s in range(2):
                        m = j * 2 + s
                        lo(a + (s + 2))
                        dve.wait_ge(bank_free[s], (a + s).turns + 1)
                        z = [s_b, s_c][s][:, :]
                        own.add(dve.tensor_tensor(z, z, y[:, m, :], ALU.mult))
                        split(z, hid_hi[:, m, :], hid_lo[:, m, :], z_done)
                steps(dve, S_GLU, KT, 2, glu, own, 4)
                own.add(dve.memset(acc[:, :], 0.0))

                def s5_out(a, j):
                    for s in range(2):
                        lo(a + (s + 2))
                        dve.wait_ge(slot_mm, (a + s).n + 1)
                        m = j * 2 + s
                        dve.tensor_copy(y[:, m, :].rearrange("p (j s) -> p j s", s=BLK),
                                        bank[s][:, :].rearrange("p (s j) -> p j s", s=BLK)).then_inc(bank_free[s], 1)
                        add_square(4, m, s)
                steps(dve, S_S5O, KT, 2, s5_out, own, 2)

            FOX_ADDS = 2 * (QB + 1) + 2 * 2 + 1 + 2 * 2
            hh_before = [0, 0, KT, 2 * KT, 3 * KT]
            own.add(dve.memset(eps[:, :], EPS))
            own.add(dve.memset(mean[:, :], 1.0 / D))
            own.add(dve.memset(acc[:, :], 0.0))
            own.add(dve.memset(ones_f[:, :], 1.0))
            own.settle()
            own.add(dve.tensor_copy(ones_r[:, :], ones_f[:, :]))
            own.add(dve.memset(blk64[:, :], 0.0))
            own.settle()
            for h in range(2):
                own.add(dve.memset(blk64[HD * h:HD * h + HD, HD * h:HD * h + HD], 1.0 / HD))
            own.settle()
            dve.sem_inc(consts, 1)
            dve.wait_ge(s5_small, 64)
            v = lambda k: s5s[:, k, :]
            tt(v(16), v(0), v(0), ALU.mult)
            tt(v(17), v(1), v(1), ALU.mult)
            tt(v(15), v(16), v(17), ALU.add)
            dve.reciprocal(v(14), v(15)).then_inc(s5_den, 1)
            dve.wait_ge(small_in, 32)
            dve.wait_ge(csil_done, 1)
            with dve.Fori(0, 2) as i:
                own.enter(i, 1)
                modulation(i)
                own.leave(2)
            scaled(amp1, SC1, "mix_pre_g", 1.0)
            own.settle()
            dve.sem_inc(mods_done, 1)

            def mixer_input(tiles):
                for k in tiles:
                    dve.wait_ge(mix_mod, 2 * k + 2)
                    wait(dve, h_done, k)
                    own.add(dve.tensor_tensor(s_a[:, :], tmp[:, k % 2, :], sq[:, k % 2, :], ALU.subtract))
                    split(s_a[:, :], hh[:, k, :], hl[:, k, :], h_done)

            modulation(2)
            scaled(gpost1, G1, "mix_post_g", 0.0)
            mixer_input(range(KT // 2))
            modulation(3)
            mixer_input(range(KT // 2, KT))
            lo(At(0))
            lo(At(1))
            modulation(4)
            scaled(amp2, SC2, "ffn_pre_g", 1.0)
            own.settle()
            for m in range(KT):
                s = m // 4
                if m % 4 == 0:
                    lo(At(S_POOL + s + 2))
                    dve.wait_ge(slot_mm, S_POOL + s + 1)
                own.settle()
                own.add(dve.tensor_scalar(y[:, m, :], bank[POOL_BANKS[m]][:, :], col("pool_scale", m), None, ALU.mult))
                own.settle()
                dve.sem_inc(x_pool, 1)
                if m % 4 == 3:
                    dve.sem_inc(bank_free[s], 1)
                add_square(0, m, m % 2)
            boundary(0)
            ffn(1, S_UP1A, conv_up, 0)
            dve.wait_ge(g2_used, 4)
            add_bias(5)
            scaled(gpost2, G2, "ffn_post_g", 0.0)
            own.add(dve.memset(wf_raw[:, :, :], 0.0))
            own.settle()
            dve.sem_inc(wf_zero, 1)
            boundary(1)
            fox()
            boundary(2)
            ffn(3, S_UP2A, silu_up, 2 * HH)
            boundary(3)
            s5()
            boundary(4)
            ffn(5, S_UP3A, silu_up, 4 * HH)
            boundary(5)

        @block.gpsimd
        def _(pool):
            pool.memset(ident[:, :], 0.0).then_inc(ident_own, 1)
            pool.wait_ge(ident_own, 1)
            pool.affine_select(out=ident[:, :], in_=ident[:, :], compare_op=ALU.not_equal, fill=1.0, base=0,
                               pattern=[[-1, P]], channel_multiplier=1).then_inc(ident_own, 1)
            pool.memset(causal[:, :], 0.0).then_inc(ident_own, 1)
            pool.wait_ge(ident_own, 3)
            pool.tensor_copy(ident_bf[:, :], ident[:, :]).then_inc(ident_own, 1)
            pool.affine_select(out=causal[:, :], in_=causal[:, :], compare_op=ALU.is_ge, fill=NEG, base=0,
                               pattern=[[-1, P]], channel_multiplier=1).then_inc(ident_own, 1)
            pool.wait_ge(ident_own, 5)
            pool.sem_inc(ident_done, 1)
            own = Tally(pool, pool_own)
            SH = [P, 4, BLK, CH]

            def tt(out_, a, b, op):
                own.add(pool.tensor_tensor(out_, a, b, op))
                own.settle()

            def ts(out_, a, s1, s2, op0, op1=None):
                own.add(pool.tensor_scalar(out_, a, s1, s2, op0) if op1 is None else
                        pool.tensor_scalar(out_, a, s1, s2, op0, op1))
                own.settle()

            own.add(pool.memset(xn[:, :, :], 0.0))
            pool.wait_ge(rcnt_in, 16)
            pool.wait_ge(rpre_done, 1)
            own.settle()
            for k in range(KT):
                g = k // 2
                w = WINDOWS[g]
                tt(xn[:, k, PAD:PAD + T], x[:, k, :], r_pre[:, :], ALU.mult)
                src, n, span, b = xn[:, k, :], PW, 1, 0
                while span < w:
                    n -= span
                    tt(pool_s[:, b, 0:n], src[:, 0:n], src[:, span:span + n], ALU.add)
                    src, span, b = pool_s[:, b, :], 2 * span, 1 - b
                at0 = PAD - w // 2
                tt(xm[:, k, :], src[:, at0:at0 + T], rcnt[:, g, :], ALU.mult)
                pool.sem_inc(xm_done, 1)

            def s5_parameters():
                v = lambda k: s5s[:, k, :]
                lam_re, lam_im, dt = v(0), v(1), v(3)
                pool.wait_ge(s5_act, 1)
                tt(v(4), lam_re, dt, ALU.mult)
                pool.sem_inc(s5_par, 1)
                tt(v(5), lam_im, dt, ALU.mult)
                ts(v(11), v(5), 1.0 / TWO_PI, None, ALU.mult)
                ts(v(11), v(11), ROUND, None, ALU.add)
                ts(v(11), v(11), -ROUND, None, ALU.add)
                for part in TWO_PI_PARTS:
                    ts(v(12), v(11), part, None, ALU.mult)
                    tt(v(5), v(5), v(12), ALU.subtract)
                ts(v(7), v(5), PI_BELOW, -PI_BELOW, ALU.min, ALU.max)
                ts(v(12), v(7), 0.0, None, ALU.max)
                ts(v(13), v(7), 0.0, None, ALU.min)
                tt(v(12), v(12), v(13), ALU.subtract)
                ts(v(8), v(12), -1.0, float(np.pi / 2), ALU.mult, ALU.add)
                pool.sem_inc(s5_par, 1)
                pool.wait_ge(s5_act, 4)
                own.add(pool.memset(pw_re[:, :, 0:1], 1.0))
                own.add(pool.memset(pw_im[:, :, 0:1], 0.0))
                tt(pw_re[:, :, 1], v(6), v(10), ALU.mult)
                tt(pw_im[:, :, 1], v(6), v(9), ALU.mult)

                def power(dst, src, mul):
                    n = dst.stop - dst.start
                    m_re = pw_re[:, :, mul:mul + 1].to_broadcast([P, PAIRS, n])
                    m_im = pw_im[:, :, mul:mul + 1].to_broadcast([P, PAIRS, n])
                    t1 = pool_s[:, 0, 0:PAIRS * n].rearrange("p (a b) -> p a b", b=n)
                    t2 = pool_s[:, 1, 0:PAIRS * n].rearrange("p (a b) -> p a b", b=n)
                    tt(t1, pw_re[:, :, src], m_re, ALU.mult)
                    tt(t2, pw_im[:, :, src], m_im, ALU.mult)
                    tt(pw_re[:, :, dst], t1, t2, ALU.subtract)
                    tt(t1, pw_re[:, :, src], m_im, ALU.mult)
                    tt(t2, pw_im[:, :, src], m_re, ALU.mult)
                    tt(pw_im[:, :, dst], t1, t2, ALU.add)
                power(slice(2, 3), slice(1, 2), 1)
                power(slice(3, 5), slice(1, 3), 2)
                power(slice(5, 9), slice(1, 5), 4)
                ts(pwn_im[:, :, :], pw_im[:, :, :], -1.0, None, ALU.mult)
                ts(v(11), pw_re[:, :, 1], -1.0, None, ALU.add)
                pool.wait_ge(s5_den, 1)
                a_im = pw_im[:, :, 1]
                tt(v(12), v(11), lam_re, ALU.mult)
                tt(v(13), a_im, lam_im, ALU.mult)
                tt(v(12), v(12), v(13), ALU.add)
                tt(z_re[:, :], v(12), v(14), ALU.mult)
                tt(v(12), a_im, lam_re, ALU.mult)
                tt(v(13), v(11), lam_im, ALU.mult)
                tt(v(12), v(12), v(13), ALU.subtract)
                tt(z_im[:, :], v(12), v(14), ALU.mult)
                pool.sem_inc(s5_par, 1)
            s5_parameters()

            def product(out_, p1, m1, p2, m2, op):
                t1 = s_b[:, :].rearrange("p (r s c) -> p r s c", r=4, s=BLK)
                t2 = s_c[:, :].rearrange("p (r s c) -> p r s c", r=4, s=BLK)
                own.add(pool.tensor_tensor(t1, p1, m1, ALU.mult))
                own.add(pool.tensor_tensor(t2, p2, m2, ALU.mult))
                own.settle()
                own.add(pool.tensor_tensor(out_.rearrange("p r (s c) -> p r s c", s=BLK), t1, t2, op))
                own.settle()

            def powers(t, i, first):
                return t[:, :, :].rearrange("p (i r) k -> p i r k", r=4)[:, i, :, first:first + BLK]\
                    .unsqueeze(3).to_broadcast(SH)

            def matrix(t, part, i):
                return t[:, part, :, :].rearrange("p (i r) c -> p i r c", r=4)[:, i, :, :]\
                    .unsqueeze(2).to_broadcast(SH)

            pool.wait_ge(s5_big, 32)
            pool.wait_ge(stat_y, 4)
            zr = z_re[:, :].unsqueeze(2).to_broadcast([P, PAIRS, CH])
            zi = z_im[:, :].unsqueeze(2).to_broadcast([P, PAIRS, CH])
            t1 = s_b[:, :].rearrange("p (r c) -> p r c", c=CH)
            t2 = s_c[:, :].rearrange("p (r c) -> p r c", c=CH)
            tt(t1, zr, b_raw[:, 0, :, :], ALU.mult)
            tt(t2, zi, b_raw[:, 1, :, :], ALU.mult)
            tt(bt[:, 0, :, :], t1, t2, ALU.subtract)
            tt(t1, zr, b_raw[:, 1, :, :], ALU.mult)
            tt(t2, zi, b_raw[:, 0, :, :], ALU.mult)
            tt(bt[:, 1, :, :], t1, t2, ALU.add)
            for k in range(BLK):
                own.add(pool.tensor_copy(rv_re[:, :, k:k + 1], pw_re[:, :, BLK - 1 - k:BLK - k]))
                own.add(pool.tensor_copy(rv_im[:, :, k:k + 1], pw_im[:, :, BLK - 1 - k:BLK - k]))
            own.add(pool.memset(w3[:, :, :], 0.0))
            own.settle()

            def q_product(dst, i, first):
                product(dst[0], powers(pw_re, i, first), matrix(cc, 0, i), powers(pw_im, i, first), matrix(cc, 1, i),
                        ALU.subtract)
                product(dst[1], powers(pwn_im, i, first), matrix(cc, 0, i), powers(pw_re, i, first), matrix(cc, 1, i),
                        ALU.subtract)

            def tables(i, p, a):
                wait(pool, k_mm, i)
                product(r_tab[:, 0, :, :], powers(rv_re, i, 0), matrix(bt, 0, i), powers(rv_im, i, 0),
                        matrix(bt, 1, i), ALU.subtract)
                product(r_tab[:, 1, :, :], powers(rv_re, i, 0), matrix(bt, 1, i), powers(rv_im, i, 0),
                        matrix(bt, 0, i), ALU.add)
                for t in range(2):
                    own.add(pool.tensor_copy(btc[:, t, :, :],
                                             bt[:, t, :, :].rearrange("p (i r) c -> p i r c", r=4)[:, i, :, :]))
                own.settle()
                pool.sem_inc(r_done, 1)
                q_product((q_tab[:, 0, :, :], q_tab[:, 1, :, :]), i, 0)
                pool.sem_inc(q_done, 1)
            for i in range(KT):
                tables(i, i % 2, None)

            pool.wait_ge(blk_mm, KT)

            def out_tables(i, p, a):
                q_product((q2[:, i, 0, :, :], q2[:, i, 1, :, :]), i, 1)
                pool.sem_inc(q2_done, 1)
            for i in range(KT):
                out_tables(i, i % 2, None)

        @block.tensor
        def _(pe):
            def passes(dst, w_h, w_l, r_h, r_l, first, last):
                pe.matmul(dst, w_h, r_h, start=first, stop=False)
                pe.matmul(dst, w_h, r_l, start=False, stop=False)
                return pe.matmul(dst, w_l, r_h, start=False, stop=last)

            def slot(a, rh, rl, kts, before=None):
                pe.wait_ge(lo_done, a.n + 1)
                wait(pe, bank_free[a.s], a.turns)
                for k in range(kts):
                    if before:
                        before(k)
                    mm = passes(bank[a.s][:, :], w_hi[:, a.s, k * P:(k + 1) * P], w_lo[:, a.s, k * P:(k + 1) * P],
                                rh[:, k, :], rl[:, k, :], k == 0, k == kts - 1)
                mm.then_inc(slot_mm, 1)

            def stat(q, k):
                pe.wait_ge(sq_done, 2 * KT * q + k + 1)
                pe.matmul(bank[PRE_BANK][:, :], mean[:, :], sq[:, k % 2, :], start=k == 0,
                          stop=k == KT - 1, skip_group_check=True).then_inc(stat_x, 1)

            def boundary(q):
                pe.wait_ge(acc_add, KT * (q + 1))
                pe.matmul(bank[POST_BANK][:, :], mean[:, :], acc[:, :], start=True, stop=True).then_inc(stat_y, 1)
                if q == 0:
                    for k in range(KT):
                        stat(q + 1, k)

            def first_input(q):
                def before(k):
                    if PRE[q]:
                        stat(q + 1, k)
                    pe.wait_ge(h_done, KT * H_SET[q] + k + 1)
                return before

            def run(first, count, rh, rl, kts, before=None):
                start = 0
                if before:
                    slot(At(first), rh, rl, kts, before)
                    slot(At(first + 1), rh, rl, kts)
                    start = 2
                with pe.Fori(0, (count - start) // 2) as i:
                    for s in range(2):
                        slot(At(first + start, i, 2) + s, rh, rl, kts)

            def hid_input(done):
                def before(k):
                    pe.wait_ge(hid_done, done + k + 1)
                return before

            def ffn(q, first, base, between=None):
                run(first, 2 * HH, hh, hl, KT, first_input(q))
                if between:
                    between()
                run(first + 2 * HH, KT, hid_hi, hid_lo, HH, hid_input(base))
                run(first + 2 * HH + KT, 2 * HH, hh, hl, KT)
                run(first + 4 * HH + KT, KT, hid_hi, hid_lo, HH, hid_input(base + HH))

            pe.wait_ge(consts, 1)
            for k in range(KT):
                stat(0, k)
            for s in range(2):
                pe.wait_ge(lo_done, S_POOL + s + 1)
                pe.wait_ge(h_done, 4 * (s + 1))
                for m in range(4):
                    g = m // 2
                    for k in range(2):
                        c = (g * 2 + k) * 2 * P + (m % 2) * P
                        mm = passes(bank[POOL_BANKS[4 * s + m]][:, :], w_hi[:, s, c:c + P], w_lo[:, s, c:c + P],
                                    hh[:, 4 * s + 2 * g + k, :], hl[:, 4 * s + 2 * g + k, :], k == 0, k == 1)
                mm.then_inc(slot_mm, 1)
            boundary(0)

            ffn(0, S_UP1A, 0)
            boundary(1)
            def scores(jj, head):
                hd = jj * 2 + head
                r = slice(HD * head, HD * head + HD)
                pe.wait_ge(qk_done, jj * 2 + 2)
                pe.wait_ge(v_done, jj + 1)
                pe.wait_ge(dsel_done, hd * 2 + 2)
                if head:
                    pe.wait_ge(pt_done, hd * 3)
                for blocks in ((0, 1, 3), (2,)):
                    for qb in blocks:
                        w = P * (qb + 1)
                        dst, qs = S_AT[qb], slice(P * qb, P * qb + P)
                        pe.matmul(dst, qk[r, 0, qs], qk[r, 2, 0:w], start=True, stop=False)
                        pe.matmul(dst, qk[r, 0, qs], qk[r, 3, 0:w], start=False, stop=False)
                        pe.matmul(dst, qk[r, 1, qs], qk[r, 2, 0:w], start=False, stop=False)
                    for qb in blocks:
                        w = P * (qb + 1)
                        dst = S_AT[qb]
                        pe.matmul(dst[:, w - P:w], ident_bf[:, :], causal[:, :], start=False, stop=False)
                        pe.matmul(dst, ones_r[:, :], dsel[:, 0, 0:w], start=False, stop=False)
                        mm = pe.matmul(dst, ones_r[:, :], dsel[:, 1, 0:w], start=False, stop=True)
                mm.then_inc(s_mm, 1)

            def transposes(jj, head):
                pe.wait_ge(p_done, jj * 2 + (head + 1))
                for kb in range(QB):
                    for qb in range(kb, QB):
                        mm = pe.transpose(T_AT[kb][:, P * (qb - kb):P * (qb - kb) + P],
                                          prob[:, P_AT[qb] + P * kb:P_AT[qb] + P * kb + P], ident[:, :])
                mm.then_inc(t_mm, 1)

            def values(jj, head):
                hd = jj * 2 + head
                pe.wait_ge(pt_done, (hd + 1) * 3)
                wait(pe, o_done, hd)
                for kb in range(QB):
                    c, w = PT_AT[kb], T - P * kb
                    mm = passes(PV_BANK[:, P * kb:T], v_hi[:, kb, :], v_lo[:, kb, :],
                                pt_hi[:, c:c + w], pt_lo[:, c:c + w], kb == 0, kb == QB - 1)
                mm.then_inc(pv_mm, 1)

            def fox_step(a, j, jj, slots, att, before=None, after_q=None):
                if slots:
                    slot(a, hh, hl, KT, before)
                if after_q:
                    after_q()
                if att:
                    scores(jj, 0)
                if slots:
                    slot(a + 1, hh, hl, KT)
                if att:
                    transposes(jj, 0)
                if slots:
                    slot(a + 2, hh, hl, KT)
                if att:
                    values(jj, 0)
                    scores(jj, 1)
                if slots:
                    slot(a + 3, hh, hl, KT)
                if att:
                    transposes(jj, 1)
                if slots:
                    for t in range(2):
                        pe.wait_ge(sqh_done, j * 2 + (t + 1))
                        pe.matmul(HS_BANK[t][:, :], blk64[:, :], sq[:, t, :], start=True, stop=True).then_inc(hs_mm, 1)
                if att:
                    values(jj, 1)
                if slots:
                    pe.wait_ge(vt_done, j + 1)
                    for tb in range(QB):
                        mm = pe.transpose(V_BANK[:, P * tb:P * tb + P], vt[:, P * tb:P * tb + P], ident[:, :])
                    mm.then_inc(vt_mm, 1)

            def forget_logits():
                pe.wait_ge(wf_split, 2)
                for k in range(KT):
                    mm = passes(bank[5][:, :], wf_hi[:, k, :], wf_lo[:, k, :], hh[:, k, :], hl[:, k, :],
                                k == 0, k == KT - 1)
                mm.then_inc(f_mm, 1)

            pe.wait_ge(ident_done, 1)
            fox_step(At(S_FOX), 0, None, True, False, first_input(1), forget_logits)
            fox_step(At(S_FOX + 4), 1, 0, True, True)
            with pe.Fori(1, KT - 1) as i:
                fox_step(At(S_FOX + 4, i, 4), i + 1, i, True, True)
            fox_step(None, None, KT - 1, False, True)

            def o_input(k):
                pe.wait_ge(o_done, 2 * (k + 1))
            run(S_FOXO, KT, hid_hi, hid_lo, KT, o_input)
            boundary(2)
            ffn(2, S_UP2A, 2 * HH)
            boundary(3)
            def rows(g):
                return slice(STATE * (g % 2), STATE * (g % 2) + STATE)

            def by_half(g):
                return 4 * (g % 2) + g // 2

            def block_products(i):
                pe.wait_ge(ub_in, (i + 1) * (16 * BLK))
                pe.wait_ge(w1_done, (i + 1) * 2)
                pe.wait_ge(w3_in, (i + 1) * (16 * BLK))
                wait(pe, blk_done, i * 3)
                for g in range(8):
                    u = ub[:, NBLK * g:NBLK * (g + 1)]
                    for t in range(2):
                        c = 4 * NBLK * t + NBLK * (g // 2)
                        pe.matmul(bank[6][rows(g), c:c + NBLK], w1[:, t, g // 2, rows(g)], u, start=True, stop=True)
                for g in range(8):
                    mm = pe.matmul(bank[7][:, NBLK * g:NBLK * (g + 1)], w3[:, by_half(g), :], ub[:, NBLK * g:NBLK * (g + 1)],
                                   start=True, stop=True)
                mm.then_inc(blk_mm, 1)

            def block_tables(i):
                pe.wait_ge(r_done, i + 1)
                pe.wait_ge(rpre_done, 5)
                wait(pe, w1_done, i * 2)
                pe.wait_ge(q_done, i + 1)
                wait(pe, kt_done, i * 2)
                for t in range(2):
                    for r4 in range(4):
                        mm = pe.transpose(bank[2 + t][:, P * r4:P * r4 + P], r_tab[:, t, r4, :], ident[:, :])
                mm.then_inc(rt_mm, 1)
                for g in range(8):
                    dst = bank[4 + g % 2][0:CH, P * (g // 2):P * (g // 2) + P]
                    for t in range(2):
                        mm = pe.matmul(dst, btc[rows(g), t, g // 2, :], q_tab[rows(g), t, g // 2, :],
                                       start=t == 0, stop=t == 1)
                mm.then_inc(k_mm, 1)

            def in_step(i, p, a):
                slot(a, hh, hl, KT, first_input(3) if isinstance(i, int) and i == 0 else None)
                if not isinstance(i, int) or i:
                    block_products(i - 1)
                block_tables(i)
            by_tile(pe, 2, S_S5I, in_step)
            block_products(KT - 1)

            def out_step(i, p, a):
                pe.wait_ge(q2_done, i + 1)
                pe.wait_ge(xc_done, (i + 1) * 2)
                if not isinstance(i, int) or i >= 2:
                    pe.wait_ge(yb_done, i - 1)
                for g in range(8):
                    for t in range(2):
                        c = NBLK * (4 * t + g // 2)
                        mm = pe.matmul(bank[4 + 2 * p + g % 2][:, NBLK * (g // 2):NBLK * (g // 2 + 1) - 1],
                                       q2[rows(g), i, t, g // 2, :], sq[rows(g), p, c:c + NBLK - 1],
                                       start=t == 0, stop=t == 1)
                mm.then_inc(out_mm, 1)

            pe.wait_ge(blk_done, 3 * KT)
            for i in range(KT):
                out_step(i, i % 2, None)

            def glu_input(k):
                pe.wait_ge(h_done, 5 * KT + k + 1)

            def z_input(k):
                pe.wait_ge(z_done, k + 1)
            run(S_GLU, KT, hh, hl, KT, glu_input)
            run(S_S5O, KT, hid_hi, hid_lo, KT, z_input)
            boundary(4)
            ffn(4, S_UP3A, 4 * HH)
            boundary(5)



def tiles(w):
    k, m = w.shape
    return np.ascontiguousarray(w.reshape(k // P, P, m // P, P).transpose(2, 1, 0, 3).reshape(m // P, P, k))


def columns(v):
    return v.reshape(-1, P).T


def features(a):
    return np.ascontiguousarray(a.T.reshape(-1, P, a.shape[0]).transpose(1, 0, 2))


def up_tiles(gate, val):
    return np.ascontiguousarray(np.stack([tiles(gate), tiles(val)], 1).reshape(2 * HT, P, D))


def down_tiles(w):
    h = FF // 2
    return np.concatenate([tiles(w[:h]), tiles(w[h:])])


def layout(**a):
    o = {}
    vecs = {"mix_pre_g": a["mix_pre_g"][0], "mix_post_g": a["mix_post_g"][0], "ffn_pre_g": a["ffn_pre_g"][0],
            "ffn_post_g": a["ffn_post_g"][0], "pool_scale": a["pool_scale"][0],
            "s5_d": a["s5_d_2"][0]}
    for i in range(2):
        vecs[f"mix_pre_{i}"] = a["mix_pre_gain_2"][i]
        vecs[f"mix_post_{i}"] = a["mix_post_gain_2"][i]
        vecs[f"ffn_pre_{i}"] = a["ffn_pre_gain_2"][i]
        vecs[f"ffn_post_{i}"] = a["ffn_post_gain_2"][i]
    gains = [np.concatenate([a[n][0], a[n][0]])[:, None] for n in ("fox_q_gain_2", "fox_k_gain_2")]
    o["vec"] = np.ascontiguousarray(np.concatenate(
        [columns(vecs[n]) for n in VECS] + [columns(a["ada_b"][0])] + gains, axis=1))
    cw = np.concatenate([a["ffn_conv_w"][0], a["ffn_conv_b"]])
    o["convw"] = np.ascontiguousarray(cw.reshape(4, 2, HT, P).transpose(3, 2, 1, 0).reshape(P, HT, 8))
    o["x"] = features(a["x"][0])
    t = np.arange(T)
    o["rcnt"] = np.stack([1.0 / (np.minimum(t + w // 2, T) - np.maximum(t - w // 2, 0)) for w in WINDOWS]
                         ).astype(np.float32)
    o["ada_w"] = np.ascontiguousarray(a["ada_w"][0].T.reshape(24, 2, P, D).transpose(0, 2, 1, 3).reshape(24, P, 2 * D))
    o["c"] = np.ascontiguousarray(a["c"])
    pw = a["pool_w"][0].reshape(2, 2, 2, P, 2 * P)
    o["pool_w"] = np.ascontiguousarray(pw.transpose(0, 3, 1, 2, 4).reshape(2, P, WK))
    up = a["ffn_w_up"][0]
    o["up1"] = up_tiles(up[:, :FF], up[:, FF:])
    o["dn1"] = down_tiles(a["ffn_w_down"][0])
    fi = a["fox_w_in_2"][0]
    four = np.stack([tiles(fi[:, i * D:(i + 1) * D]) for i in range(4)], 1)
    o["fox_in"] = np.ascontiguousarray(four.reshape(4 * KT, P, D))
    o["fox_f"] = np.ascontiguousarray(fi[:, 4 * D:].reshape(KT, P, HEADS).transpose(1, 0, 2))
    o["fox_bf"] = np.ascontiguousarray(a["fox_b_f_2"][0][:, None])
    o["fox_out"] = tiles(a["fox_w_out_2"][0])
    for n in ("lam_re", "lam_im"):
        o[f"s5_{n}"] = np.ascontiguousarray(a[f"s5_{n}_2"][0].reshape(PAIRS, 2, STATE).transpose(1, 2, 0)
                                            .reshape(P, PAIRS))
    o["s5_log_dt"] = np.ascontiguousarray(a["s5_log_dt_2"][0].reshape(PAIRS, 2).T)
    b = np.stack([a["s5_b_re_2"][0], a["s5_b_im_2"][0]])
    o["s5_b"] = np.ascontiguousarray(b.reshape(2, PAIRS, 2, STATE, CH).transpose(2, 3, 0, 1, 4)
                                     .reshape(P, 2, PAIRS, CH))
    c = np.stack([a["s5_c_re_2"][0], a["s5_c_im_2"][0]])
    o["s5_c"] = np.ascontiguousarray(c.reshape(2, PAIRS, 2, CH, STATE).transpose(2, 4, 0, 1, 3)
                                     .reshape(P, 2, PAIRS, CH))
    o["s5_w"] = np.concatenate([tiles(a[f"s5_w_{n}_2"][0]) for n in ("in", "glu", "out")])
    for i in range(2):
        o[f"up{i + 2}"] = up_tiles(a["ffn_w_gate_2"][i], a["ffn_w_up_2"][i])
        o[f"dn{i + 2}"] = down_tiles(a["ffn_w_down_2"][i])
    return o


def kernel(**inputs):
    import concourse.bacc as bacc
    from concourse.bass_utils import run_bass_kernel_spmd

    arrays = layout(**{k: np.asarray(v) for k, v in inputs.items()})
    nc = bacc.Bacc("TRN2", target_bir_lowering=False, num_devices=1)
    dram = {n: nc.dram_tensor(f"in_{n}", v.shape, mybir.dt.from_np(v.dtype), kind="ExternalInput").ap()
            for n, v in arrays.items()}
    out = nc.dram_tensor("out", (P, KT, T), F32, kind="ExternalOutput").ap()
    build(nc, dram, out)
    r = run_bass_kernel_spmd(nc, [{f"in_{n}": v for n, v in arrays.items()}], core_ids=[0])
    got = np.asarray(r.results[0]["out"])
    return np.ascontiguousarray(got.transpose(1, 0, 2).reshape(D, T).T)[None]
```

```python
from contextlib import ExitStack

import numpy as np
import concourse.bass as bass
from concourse import mybir

P = 128
F32 = mybir.dt.float32
F32R = mybir.dt.float32r
BF16 = mybir.dt.bfloat16
ALU = mybir.AluOpType
ACT = mybir.ActivationFunctionType

D = 1024
T = 512
KT = D // P
FF = 2816
HT = FF // P
HH = HT // 2
EPS = 1e-6
TWO_PI = 2 * np.pi
TWO_PI_PARTS = (6.28125, 0.0019350051879882812, float(np.float32(TWO_PI - 6.28125 - 0.0019350051879882812)))
ROUND = 1.5 * 2 ** 23
PI_BELOW = 3.1415925
WINDOWS = (2, 4, 8, 16)
PAD = max(WINDOWS) // 2
HEADS = 16
HD = D // HEADS
QB = T // P
NEG = -1e30
BLK = 8
NBLK = T // BLK
CH = 16
GROUPS = D // CH
PAIRS = GROUPS // 2
STATE = 64

VECS = ["mix_pre_g", "mix_post_g", "ffn_pre_g", "ffn_post_g", "pool_scale",
        "mix_pre_0", "mix_pre_1", "mix_post_0", "mix_post_1",
        "ffn_pre_0", "ffn_pre_1", "ffn_post_0", "ffn_post_1", "s5_d"]
VCOL = {name: KT * i for i, name in enumerate(VECS)}
ADA_B = KT * len(VECS)
QK_GAIN = ADA_B + 6 * KT
NVEC = QK_GAIN + 2
SH1, SC1, G1, SH2, SC2, G2 = (KT * i for i in range(6))

S_POOL = 0
S_UP1A = S_POOL + 2
S_DN1A = S_UP1A + 2 * HH
S_UP1B = S_DN1A + KT
S_DN1B = S_UP1B + 2 * HH
S_FOX = S_DN1B + KT
S_FOXO = S_FOX + 4 * KT
S_UP2A = S_FOXO + KT
S_DN2A = S_UP2A + 2 * HH
S_UP2B = S_DN2A + KT
S_DN2B = S_UP2B + 2 * HH
S_S5I = S_DN2B + KT
S_GLU = S_S5I + KT
S_S5O = S_GLU + KT
S_UP3A = S_S5O + KT
S_DN3A = S_UP3A + 2 * HH
S_UP3B = S_DN3A + KT
S_DN3B = S_UP3B + 2 * HH
SLOTS = S_DN3B + KT
WK = KT * P
WH = HH * P


def slot_width(n):
    for s in (S_DN1A, S_DN1B, S_DN2A, S_DN2B, S_DN3A, S_DN3B):
        if s <= n < s + KT:
            return WH
    return WK


class Tally:

    def __init__(self, eng, sem):
        self.eng, self.sem, self.n, self.loop = eng, sem, 0, None

    def add(self, ins):
        ins.then_inc(self.sem, 1)
        self.n += 1

    def settle(self):
        self.eng.wait_ge(self.sem, self.n if self.loop is None else self.loop[0] * self.loop[1] + self.n)

    def enter(self, i, per, first=0):
        self.n -= first * per
        self.loop = (i, per, self.n)

    def leave(self, end):
        i, per, start = self.loop
        assert self.n - start == per, (self.n - start, per)
        self.n = start + per * end
        self.loop = None


class At:

    def __init__(self, n0, i=0, per=0):
        self.n0, self.i, self.per = n0, i, per
        self.n = n0 + i * per if per else n0
        self.s = n0 % 2
        self.turns = n0 // 2 + (i * (per // 2) if per else 0)

    def __add__(self, k):
        return At(self.n0 + k, self.i, self.per)


def steps(eng, first, count, per, body, tally=None, adds=0, lead=0):
    trips = count // per
    for i in range(lead):
        body(At(first + i * per), i)
    with eng.Fori(lead, trips - 1) as i:
        if tally:
            tally.enter(i, adds, lead)
        body(At(first, i, per), i)
        if tally:
            tally.leave(trips - 1)
    body(At(first + (trips - 1) * per), trips - 1)


def by_tile(eng, lead, first, body, tally=None, adds=0):
    for i in range(lead):
        body(i, i % 2, At(first + i))
    trips = (KT - lead) // 2
    with eng.Fori(0, trips) as t:
        if tally:
            tally.enter(t, 2 * adds)
        for p in range(2):
            body(t * 2 + (lead + p), (lead + p) % 2, At(first + lead + p, t, 2))
        if tally:
            tally.leave(trips)
    for i in range(lead + 2 * trips, KT):
        body(i, i % 2, At(first + i))


def build(nc, dram, out):
    with ExitStack() as ctx:
        top = [-(-nc.sbuf_base // 64) * 64]

        def at(name, shape, dt, offset):
            return nc.alloc_sbuf_tensor_at(name, [P] + shape, dt, offset=offset)

        def sb(name, shape, dt=F32):
            offset = top[0]
            top[0] += -(-int(np.prod(shape)) * (2 if dt == BF16 else 4) // 64) * 64
            assert top[0] <= nc.sbuf_usable_end, (name, top[0])
            return at(name, shape, dt, offset)

        def region(cols):
            offset = top[0]
            top[0] += 4 * cols
            assert top[0] <= nc.sbuf_usable_end, top[0]
            return offset

        def sem(name):
            return ctx.enter_context(nc.semaphore(name))

        x = sb("x", [KT, T])
        hh_at = top[0]
        hh = sb("hh", [KT, T], F32R)
        hl = sb("hl", [KT, T], F32R)
        raw = sb("raw", [2, WH])
        w_hi = sb("w_hi", [2, WH], F32R)
        w_lo = sb("w_lo", [2, WH], F32R)
        vec = sb("vec", [NVEC])
        convw = sb("convw", [HT, 8])
        mods = sb("mods", [6 * KT])
        amp1 = sb("amp1", [KT])
        amp2 = sb("amp2", [KT])
        gpost1 = sb("gpost1", [KT])
        gpost2 = sb("gpost2", [KT])
        dots = sb("dots", [KT])
        eps = sb("eps", [1])
        scrap = sb("scrap", [1])
        mean = sb("mean", [P])
        r_pre = sb("r_pre", [T])
        rpost_at = top[0]
        r_post = sb("r_post", [T])
        lnr = sb("lnr", [T])
        acc = sb("acc", [T])
        sq = sb("sq", [2, T])
        tmp = sb("tmp", [2, T])
        s_a = sb("s_a", [T])
        s_b = sb("s_b", [T])
        s_c = sb("s_c", [T])
        s_p = sb("s_p", [T])
        y_at = region(KT * T)
        hid_at = region(2 * HH * T)
        z_at = region(4 * 2 * WK)
        y = at("y", [KT, T], F32, y_at)
        hid_hi = at("hid_hi", [HH, T], F32R, hid_at)
        hid_lo = at("hid_lo", [HH, T], F32R, hid_at + 4 * HH * T)
        ada_w = at("ada_w", [4, 2 * D], F32, hid_at)
        csil = at("csil", [D], F32, hid_at + 4 * 8 * D)
        g2_w = at("g2_w", [3, 2 * D], F32, z_at)
        g2_csil = at("g2_csil", [D], F32, z_at + 4 * 7 * D)
        rcnt = at("rcnt", [4, T], F32, z_at)
        PW = T + 2 * PAD
        pool_s = at("pool_s", [2, PW], F32, z_at + 4 * 4 * T)
        xn = at("xn", [KT, PW], F32, z_at + 4 * (4 * T + 2 * PW))
        xm = y
        ident = sb("ident", [P])
        blk64 = sb("blk64", [P])
        ones_f = sb("ones_f", [P])
        ident_bf = sb("ident_bf", [P], BF16)
        causal = sb("causal", [P], BF16)
        ones_r = sb("ones_r", [P], F32R)
        qk_gain = sb("qk_gain", [2])
        bf_col = sb("bf_col", [1])
        nmax = sb("nmax", [QB])
        rsum = sb("rsum", [QB])
        rinv = sb("rinv", [QB])
        qk = at("qk", [4, T], F32R, y_at)
        zc = z_at
        v_hi = at("v_hi", [QB, P], F32R, zc)
        v_lo = at("v_lo", [QB, P], F32R, zc + 4 * T)
        gsig = at("gsig", [T], F32, zc + 8 * T)
        dsel = at("dsel", [2, T], F32R, zc + 12 * T)
        NP_ = P * QB * (QB + 1) // 2
        prob = at("prob", [NP_], F32, zc + 20 * T)
        pt_hi = at("pt_hi", [NP_], F32R, zc + 20 * T + 4 * NP_)
        pt_lo = at("pt_lo", [NP_], F32R, zc + 20 * T + 8 * NP_)
        assert 20 * T + 12 * NP_ <= 4 * 8 * WK
        wf_raw = at("wf_raw", [KT, P], F32, zc + 20 * T)
        wf_hi = at("wf_hi", [KT, P], F32R, zc + 20 * T + 4 * WK)
        wf_lo = at("wf_lo", [KT, P], F32R, zc + 20 * T + 8 * WK)
        tail = hid_at + 4 * KT * T
        qf = at("qf", [2, T], F32, tail)
        vt = at("vt", [T], F32, tail + 8 * T)
        tail = hid_at + 4 * (HH + KT) * T
        c_hi = at("c_hi", [T], F32R, tail)
        c_lo = at("c_lo", [T], F32R, tail + 4 * T)
        cums = at("cums", [T], F32, tail + 8 * T)
        LEVELS = 3
        factors = at("factors", [LEVELS + 1, 3, PAIRS], F32, rpost_at)
        terms = at("terms", [2, NBLK // 2, 2 * PAIRS], F32, hh_at)
        ones_row = ones_f[:, 0:PAIRS]
        NPW = BLK + 1
        pw_re = sb("pw_re", [PAIRS, NPW])
        pw_im = sb("pw_im", [PAIRS, NPW])
        pwn_im = sb("pwn_im", [PAIRS, NPW])
        z_re = sb("z_re", [PAIRS])
        z_im = sb("z_im", [PAIRS])
        s5s = at("s5s", [20, PAIRS], F32, z_at + 4 * (4 * T + (2 + KT) * PW))
        QW = NPW * CH
        xs = at("xs", [NBLK, 2 * PAIRS], F32, z_at)
        yb = at("yb", [KT, T], F32, z_at + 4 * KT * T)
        b_raw = at("b_raw", [2, PAIRS, CH], F32, z_at)
        cc = at("cc", [2, PAIRS, CH], F32, z_at + 4 * 2 * PAIRS * CH)
        bt = at("bt", [2, PAIRS, CH], F32, z_at + 8 * 2 * PAIRS * CH)
        hc = z_at + 12 * 2 * PAIRS * CH
        btc = at("btc", [2, 4, CH], F32, hc)
        r_tab = at("r_tab", [2, 4, P], F32, hc + 4 * 8 * CH)
        w1_new = at("w1_new", [2, 4, P], F32, hc + 4 * (8 * CH + 8 * P))
        kt = at("kt", [8, P], F32, hc + 4 * (8 * CH + 16 * P))
        q_tab = at("q_tab", [2, 4, QW], F32, hc + 4 * (8 * CH + 24 * P))
        prod = at("prod", [4, QW], F32, hc + 4 * (8 * CH + 24 * P + 8 * QW))
        prod_b = at("prod_b", [PAIRS, CH], F32, hc + 4 * (8 * CH + 24 * P + 8 * QW))
        assert hc + 4 * (8 * CH + 24 * P + 12 * QW) <= z_at + 4 * 8 * WK
        q2 = at("q2", [KT, 2, 4, QW], F32, hid_at)
        w1 = at("w1", [2, 2, 4, P], F32, hid_at + 4 * (KT - 2) * 8 * QW)
        w3 = at("w3", [2, 8, P], F32, hid_at + 4 * ((KT - 2) * 8 * QW + 16 * P))
        assert (KT - 2) * 8 * QW + 32 * P <= 2 * HH * T
        ub = [s_a, s_b]
        w1_dram = nc.dram_tensor("w1_scratch", (KT, P, 8 * P), F32, kind="Internal").ap()
        w3_dram = nc.dram_tensor("w3_scratch", (KT, P, 8, P), F32, kind="Internal").ap()
        q_dram = nc.dram_tensor("q_scratch", (KT, P, 8 * QW), F32, kind="Internal").ap()
        u_dram = nc.dram_tensor("u_scratch", (KT, P, T), F32, kind="Internal").ap()
        y_dram = nc.dram_tensor("y_scratch", (KT, P, T), F32, kind="Internal").ap()

        bank = [ctx.enter_context(nc.psum_tensor(f"bank{i}", [P, T], F32)) for i in range(8)]
        POST_BANK, PRE_BANK = 2, 3
        POOL_BANKS = [0, 2, 3, 4, 1, 5, 6, 7]

        small_in = sem("small_in")
        x_in = sem("x_in")
        x_pool = sem("x_pool")
        rcnt_in = sem("rcnt_in")
        raw_full = [sem("raw_full0"), sem("raw_full1")]
        hi_done = sem("hi_done")
        lo_done = sem("lo_done")
        slot_mm = sem("slot_mm")
        bank_free = [sem("bank_free0"), sem("bank_free1")]
        ada_full = [sem(f"ada_full{i}") for i in range(4)]
        ada_used = sem("ada_used")
        c_in = sem("c_in")
        xm_done = sem("xm_done")
        mix_mod = sem("mix_mod")
        s5_den = sem("s5_den")
        s5_par = sem("s5_par")
        g2_in = [sem(f"g2_in{i}") for i in range(4)]
        g2_used = sem("g2_used")
        consts = sem("consts")
        csil_done = sem("csil_done")
        sq_done = sem("sq_done")
        acc_add = sem("acc_add")
        stat_x = sem("stat_x")
        stat_y = sem("stat_y")
        rpre_done = sem("rpre_done")
        rpost_done = sem("rpost_done")
        x_upd = sem("x_upd")
        hh_done = sem("hh_done")
        h_done = sem("h_done")
        conv_mid = sem("conv_mid")
        act_done = sem("act_done")
        hid_done = sem("hid_done")
        mods_done = sem("mods_done")
        dve_own = sem("dve_own")
        act_own = sem("act_own")
        stored = sem("stored")
        ident_own = sem("ident_own")
        ident_done = sem("ident_done")
        s5_small = sem("s5_small")
        s5_big = sem("s5_big")
        s5_act = sem("s5_act")
        pool_own = sem("pool_own")
        r_done = sem("r_done")
        q_done = sem("q_done")
        rt_mm = sem("rt_mm")
        k_mm = sem("k_mm")
        w1_done = sem("w1_done")
        kt_done = sem("kt_done")
        u_out = sem("u_out")
        ub_in = [sem("ub_in0"), sem("ub_in1")]
        w1_in = [sem("w1_in0"), sem("w1_in1")]
        w3_in = [sem("w3_in0"), sem("w3_in1")]
        w3_zero = sem("w3_zero")
        zeros_done = sem("zeros_done")
        w1_out = sem("w1_out")
        w3_out = sem("w3_out")
        q_out = sem("q_out")
        blk_mm = sem("blk_mm")
        blk_done = sem("blk_done")
        rec_done = sem("rec_done")
        q2_in = [sem("q2_in0"), sem("q2_in1")]
        xc_done = sem("xc_done")
        out_mm = sem("out_mm")
        yb_done = sem("yb_done")
        y_out = [sem("y_out0"), sem("y_out1")]
        yt_in = [sem("yt_in0"), sem("yt_in1")]
        pre_gelu = sem("pre_gelu")
        gelu_done = sem("gelu_done")
        z_done = sem("z_done")
        wf_zero = sem("wf_zero")
        wf_in = sem("wf_in")
        wf_split = sem("wf_split")
        f_mm = sem("f_mm")
        f_act = sem("f_act")
        z_ready = sem("z_ready")
        sqh_done = sem("sqh_done")
        hs_mm = sem("hs_mm")
        hr_done = sem("hr_done")
        qk_done = sem("qk_done")
        vt_done = sem("vt_done")
        vt_mm = sem("vt_mm")
        vh_done = sem("vh_done")
        v_done = sem("v_done")
        g_done = sem("g_done")
        dsel_done = sem("dsel_done")
        s_mm = sem("s_mm")
        mx_done = sem("mx_done")
        exp_done = sem("exp_done")
        p_done = sem("p_done")
        t_mm = sem("t_mm")
        pth_done = sem("pth_done")
        pt_done = sem("pt_done")
        pv_mm = sem("pv_mm")
        o_done = sem("o_done")

        block = ctx.enter_context(nc.Block())

        def wait(eng, s, v):
            assert isinstance(v, int) or v.min_val > 0
            if not (isinstance(v, int) and v <= 0):
                eng.wait_ge(s, v)

        def col(name, k):
            return vec[:, VCOL[name] + k:VCOL[name] + k + 1]

        POST = [lambda k: gpost1[:, k:k + 1], lambda k: gpost2[:, k:k + 1],
                lambda k: col("mix_post_0", k), lambda k: col("ffn_post_0", k),
                lambda k: col("mix_post_1", k), lambda k: col("ffn_post_1", k)]
        PRE = [None, lambda k: col("mix_pre_0", k), lambda k: col("ffn_pre_0", k),
               lambda k: col("mix_pre_1", k), lambda k: col("ffn_pre_1", k)]
        H_SET = [1, 2, 3, 4, 6]

        S_AT = [bank[2][:, 0:P], bank[3][:, 0:2 * P], bank[2][:, P:4 * P], bank[4][:, :]]
        P_AT = [0, P, 3 * P, 6 * P]
        T_AT = [bank[5][:, :], bank[6][:, 0:3 * P], bank[3][:, 2 * P:4 * P], bank[6][:, 3 * P:4 * P]]
        PT_AT = [0, 4 * P, 8 * P, 7 * P]
        T_PARTS = [(bank[5][:, :], 0, 4 * P), (bank[6][:, :], 4 * P, 4 * P), (bank[3][:, 2 * P:4 * P], 8 * P, 2 * P)]
        PV_BANK, V_BANK = bank[7], bank[5]
        HS_BANK = [bank[2], bank[4]]

        def u_back(eng, i, p, tokens):
            eng.wait_ge(u_out, (i + 1) * 16)
            src = u_dram[i].rearrange("(g c) (s j) -> s c g j", c=CH, s=BLK)
            for t in tokens:
                eng.dma_start(ub[p][CH * t:CH * t + CH, :].rearrange("p (g j) -> p g j", g=8), src[t])\
                   .then_inc(ub_in[p], 16)

        def y_back(eng, i, p, groups):
            eng.wait_ge(y_out[p], (i - p) * 8 + 16)
            if not isinstance(i, int) or i >= 2:
                eng.wait_ge(pre_gelu, i - 1)
            src = y_dram[i].rearrange("(s c) (g j) -> g c s j", c=CH, g=8)
            for g in groups:
                eng.dma_start(tmp[CH * g:CH * g + CH, p, :].rearrange("p (s j) -> p s j", s=BLK), src[g])\
                   .then_inc(yt_in[p], 16)

        @block.sync
        def _(sp):
            sp.dma_start(vec[:, :], dram["vec"]).then_inc(small_in, 16)
            sp.dma_start(convw[:, :, :], dram["convw"]).then_inc(small_in, 16)
            sp.dma_start(x[:, :, :], dram["x"]).then_inc(x_in, 16)
            sp.dma_start(csil[:, :], dram["c"].to_broadcast([P, D])).then_inc(c_in, 16)
            for k, name in enumerate(("s5_lam_re", "s5_lam_im")):
                sp.dma_start(s5s[:, k, :], dram[name]).then_inc(s5_small, 16)
            for h in range(2):
                sp.dma_start(s5s[STATE * h:STATE * h + STATE, 2, :],
                             dram["s5_log_dt"][h:h + 1, :].to_broadcast([STATE, PAIRS])).then_inc(s5_small, 16)
            sp.dma_start(rcnt[:, :, :], dram["rcnt"].unsqueeze(0).to_broadcast([P, 4, T])).then_inc(rcnt_in, 16)

            def load(a, src, width):
                wait(sp, hi_done, a.n - 1)
                wait(sp, lo_done, a.n - 1)
                sp.dma_start(raw[:, a.s, 0:width], src).then_inc(raw_full[a.s], 16)

            def loads(first, count, src, src0, width):
                with sp.Fori(0, count // 2) as i:
                    for s in range(2):
                        load(At(first, i, 2) + s, src[i * 2 + (src0 + s)], width)

            def load_ffn(first, up, dn, skip=0):
                loads(first + skip, 2 * HH - skip, up, skip, WK)
                loads(first + 2 * HH, KT, dn, 0, WH)
                if first == S_UP1A:
                    sp.wait_ge(g2_used, 1)
                    sp.dma_start(g2_w[:, 0, :], dram["ada_w"][4 * 5 + 3]).then_inc(g2_in[3], 16)
                loads(first + 2 * HH + KT, 2 * HH, up, 2 * HH, WK)
                loads(first + 4 * HH + KT, KT, dn, KT, WH)

            for s in range(2):
                load(At(S_POOL + s), dram["pool_w"][s], WK)
            for b in range(4):
                sp.dma_start(ada_w[:, b, :], dram["ada_w"][b]).then_inc(ada_full[b], 16)
            with sp.Fori(0, 4) as i:
                for b in range(4):
                    sp.wait_ge(ada_used, i * 4 + b + 1)
                    sp.dma_start(ada_w[:, b, :], dram["ada_w"][i * 4 + b + 4]).then_inc(ada_full[b], 16)
            for s in range(2):
                load(At(S_UP1A + s), dram["up1"][s], WK)
            sp.wait_ge(h_done, KT)
            sp.wait_ge(s5_par, 3)
            sp.dma_start(g2_csil[:, :], dram["c"].to_broadcast([P, D])).then_inc(c_in, 16)
            for b in range(3):
                sp.dma_start(g2_w[:, b, :], dram["ada_w"][4 * 5 + b]).then_inc(g2_in[b], 16)
            load_ffn(S_UP1A, dram["up1"], dram["dn1"], skip=2)
            for s in range(2):
                load(At(S_FOX + s), dram["fox_in"][s], WK)
            sp.wait_ge(wf_zero, 1)
            sp.dma_start(wf_raw[:, :, 0:HEADS], dram["fox_f"]).then_inc(wf_in, 16)
            sp.dma_start(bf_col[0:HEADS, :], dram["fox_bf"]).then_inc(wf_in, 16)
            loads(S_FOX + 2, 4 * KT - 2, dram["fox_in"], 2, WK)
            loads(S_FOXO, KT, dram["fox_out"], 0, WK)
            for s in range(2):
                load(At(S_UP2A + s), dram["up2"][s], WK)
            sp.wait_ge(stat_y, 3)
            sp.dma_start(b_raw[:, :, :, :], dram["s5_b"]).then_inc(s5_big, 16)
            sp.dma_start(cc[:, :, :, :], dram["s5_c"]).then_inc(s5_big, 16)
            sp.wait_ge(zeros_done, 1)
            for i in range(KT):
                sp.dma_start(w3_dram[i], kt[:, :, :]).then_inc(w3_zero, 16)
            load_ffn(S_UP2A, dram["up2"], dram["dn2"], skip=2)
            for s in range(2):
                load(At(S_S5I + s), dram["s5_w"][s], WK)
            sp.wait_ge(slot_mm, S_S5I)
            sp.wait_ge(q_out, 16 * KT)
            sp.wait_ge(w1_out, 16 * BLK * KT)
            sp.wait_ge(w3_out, 16 * BLK * KT)
            q_rows = q_dram.rearrange("i p c -> p i c")
            q_cols = q2[:, :, :, :, :].rearrange("p i a b c -> p i (a b c)")

            def tables_in(i, p):
                if not isinstance(i, int) or i >= 2:
                    sp.wait_ge(blk_mm, i - 1)
                sp.dma_start(w1[:, p, :, :, :].rearrange("p a b c -> p (a b c)"), w1_dram[i]).then_inc(w1_in[p], 16)
                sp.dma_start(w3[:, p, :, :], w3_dram[i]).then_inc(w3_in[p], 16)

            def s5_in_step(i, p, a):
                sp.wait_ge(bank_free[p], a.turns + 1)
                sp.dma_start(u_dram[i], y[:, i, :]).then_inc(u_out, 16)
                u_back(sp, i, p, range(0, BLK // 2))
                load(a + 3, dram["s5_w"][i + 3], WK)
                if not isinstance(i, int) or i < KT - 1:
                    tables_in(i + 1, 1 - p)
            tables_in(0, 0)
            load(At(S_S5I + 2), dram["s5_w"][2], WK)
            by_tile(sp, 1, S_S5I, s5_in_step)
            sp.dma_start(q_cols[:, 0:KT - 2, :], q_rows[:, 0:KT - 2, :]).then_inc(q2_in[0], 16)
            sp.wait_ge(blk_mm, KT)
            sp.dma_start(q_cols[:, KT - 2:KT, :], q_rows[:, KT - 2:KT, :]).then_inc(q2_in[1], 16)

            def s5_out_step(i, p, a):
                sp.wait_ge(yb_done, i + 1)
                sp.dma_start(y_dram[i], yb[:, i, :]).then_inc(y_out[p], 16)
                if not isinstance(i, int) or i >= 1:
                    y_back(sp, i - 1, 1 - p, range(4))
            by_tile(sp, 4, 0, s5_out_step)
            y_back(sp, KT - 1, (KT - 1) % 2, range(4))
            load(At(S_GLU + 3), dram["s5_w"][KT + 3], WK)
            loads(S_GLU + 4, 2 * KT - 4, dram["s5_w"], KT + 4, WK)
            load_ffn(S_UP3A, dram["up3"], dram["dn3"])
            for k in range(KT):
                sp.wait_ge(x_upd, 5 * KT + k + 1)
                sp.dma_start(out[:, k, :], x[:, k, :]).then_inc(stored, 16)
            sp.wait_ge(stored, 16 * KT)

        @block.scalar
        def _(act):
            own = Tally(act, act_own)

            def hi(a):
                if a.n0 >= SLOTS:
                    return
                width = slot_width(a.n0)
                act.wait_ge(raw_full[a.s], (a.turns + 1) * 16)
                wait(act, slot_mm, a.n - 1)
                act.activation(w_hi[:, a.s, 0:width], raw[:, a.s, 0:width], ACT.Copy).then_inc(hi_done, 1)

            def rsqrt(dst, b, done):
                own.add(act.activation(lnr[:, :], bank[b][:, :], ACT.Ln, bias=eps[:, 0:1]))
                own.settle()
                act.activation(dst[:, :], lnr[:, :], ACT.Exp, scale=-0.5).then_inc(done, 1)

            def squares_x(q, k):
                wait(act, stat_x, KT * q + k - 1 if k >= 2 else 0)
                act.activation(sq[:, k % 2, :], x[:, k, :], ACT.Square).then_inc(sq_done, 1)

            def prime(func):
                own.settle()
                own.add(act.activation(scrap[:, :], eps[:, :], func))

            def boundary(q):
                prime(ACT.Ln)
                act.wait_ge(stat_y, q + 1)
                rsqrt(r_post, POST_BANK, rpost_done)
                if q == len(POST) - 1:
                    return
                for k in range(KT):
                    act.wait_ge(x_upd, KT * q + k + 1)
                    if PRE[q]:
                        act.activation(hh[:, k, :], x[:, k, :], ACT.Copy, scale=PRE[q](k)).then_inc(hh_done, 1)
                    squares_x(q + 1, k)
                prime(ACT.Ln)
                act.wait_ge(stat_x, KT * (q + 2))
                rsqrt(r_pre, PRE_BANK, rpre_done)

            def y_square(q, a, m, k2):
                act.wait_ge(bank_free[a.s], a.turns + 1)
                act.wait_ge(acc_add, m + KT * q - 1) if q else None
                act.activation(sq[:, k2, :], y[:, m, :], ACT.Square).then_inc(sq_done, 1)

            def down(q, first):
                def first_half(a, j):
                    for s in range(2):
                        hi(a + (s + 2))

                def second_half(a, j):
                    for s in range(2):
                        hi(a + (s + 2))
                        y_square(q, a + s, j * 2 + s, s)
                return first_half, second_half

            def conv_up(half, base):
                def body(a, j):
                    i = j + half * HH
                    for s in range(2):
                        hi(a + (s + 2))
                        act.wait_ge(slot_mm, (a + s).n + 1)
                        wait(act, hid_done, base + j)
                        act.activation([s_a, s_c][s][:, :], bank[s][:, :], ACT.Identity,
                                       scale=convw[:, i, 4 * s + 1:4 * s + 2],
                                       bias=convw[:, i, 4 * s + 3:4 * s + 4]).then_inc(conv_mid, 1)
                        if s == 0:
                            act.wait_ge(bank_free[0], (a + 0).turns + 1)
                            act.activation(s_b[:, :], s_a[:, :], ACT.Gelu_apprx_tanh).then_inc(act_done, 1)
                return body

            def silu_up(half, base):
                def body(a, j):
                    hi(a + 2)
                    act.wait_ge(bank_free[0], a.turns + 1)
                    act.activation(s_b[:, :], s_a[:, :], ACT.Silu).then_inc(act_done, 1)
                    hi(a + 3)
                return body

            def store_tables(i):
                flat = "p a b -> p (a b)"
                act.wait_ge(rt_mm, i + 1)
                wait(act, w1_out, i * (16 * BLK))
                for t in range(2):
                    act.activation(w1_new[:, t, :, :].rearrange(flat), bank[4 + t][:, :], ACT.Copy)\
                       .then_inc(w1_done, 1)
                act.wait_ge(k_mm, i + 1)
                wait(act, w3_out, i * (16 * BLK))
                for t in range(2):
                    act.activation(kt[0:CH, 4 * t:4 * t + 4, :].rearrange(flat), bank[6 + t][0:CH, :], ACT.Copy)\
                       .then_inc(kt_done, 1)
                act.wait_ge(q_done, i + 1)
                act.dma_start(q_dram[i], q_tab[:, :, :, :].rearrange("p a b c -> p (a b c)")).then_inc(q_out, 16)
                act.wait_ge(w1_done, i * 2 + 2)
                for k in range(BLK):
                    row = CH * (BLK - 1 - k)
                    act.dma_start(w1_dram[i][row:row + CH], w1_new[CH * k:CH * k + CH, :, :, :].rearrange(
                        "p a b c -> p (a b c)")).then_inc(w1_out, 16)
                act.wait_ge(kt_done, i * 2 + 2)
                act.wait_ge(w3_zero, 16 * KT)
                for t in range(BLK):
                    act.dma_start(w3_dram[i][CH * t:CH * t + CH, :, CH * t:P], kt[0:CH, :, 0:P - CH * t])\
                       .then_inc(w3_out, 16)

            def with_tables(body, first):
                def both(a, j):
                    body(a, j)
                    store_tables(j + first)
                return both

            def ffn(q, first, up, base):
                lo_half, hi_half = down(q, first)
                tables = q == 3
                if tables:
                    lo_half, hi_half = with_tables(lo_half, 0), with_tables(hi_half, KT // 2)
                steps(act, first, 2 * HH, 2, up(0, base), lead=1)
                if q == 1:
                    act.wait_ge(c_in, 32)
                    act.activation(g2_csil[:, :], g2_csil[:, :], ACT.Silu).then_inc(csil_done, 1)
                steps(act, first + 2 * HH, KT, 2, lo_half, lead=1 if tables else 0)
                steps(act, first + 2 * HH + KT, 2 * HH, 2, up(1, base + HH))
                steps(act, first + 4 * HH + KT, KT, 2, hi_half)

            def attend(jj, head, exp=False, pt=False):
                hd = jj * 2 + head
                if exp:
                    act.wait_ge(mx_done, hd + 1)
                    for qb in range(QB):
                        w = P * (qb + 1)
                        e = act.activation(prob[:, P_AT[qb]:P_AT[qb] + w], S_AT[qb], ACT.Exp,
                                           bias=nmax[:, qb:qb + 1], accum_out=rsum[:, qb:qb + 1])
                    e.then_inc(exp_done, 1)
                if pt:
                    act.wait_ge(t_mm, hd + 1)
                    wait(act, pv_mm, hd)
                    for b, c, w in T_PARTS:
                        act.activation(pt_hi[:, c:c + w], b, ACT.Copy).then_inc(pth_done, 1)

            def fox_step(a, j, jj, kk, forget=None):
                if kk is not None:
                    attend(kk, 1, pt=True)
                if j is not None:
                    hi(a + 2)
                    act.wait_ge(bank_free[0], a.turns + 1)
                    act.activation(sq[:, 0, :], qf[:, 0, :], ACT.Square).then_inc(sqh_done, 1)
                if jj is not None:
                    act.wait_ge(vt_mm, jj + 1)
                    if kk is not None:
                        act.wait_ge(pv_mm, kk * 2 + 2)
                    act.activation(v_hi[:, :, :].rearrange("p a b -> p (a b)"), V_BANK[:, :], ACT.Copy).then_inc(vh_done, 1)
                    act.wait_ge(bank_free[1], (At(S_FOX + 3, jj, 4)).turns + 1)
                    if kk is not None:
                        act.wait_ge(o_done, kk * 2 + 2)
                    act.activation(gsig[:, :], s_a[:, :], ACT.Sigmoid).then_inc(g_done, 1)
                    attend(jj, 0, exp=True)
                if j is not None:
                    hi(a + 3)
                    act.wait_ge(bank_free[1], (a + 1).turns + 1)
                    act.activation(sq[:, 1, :], qf[:, 1, :], ACT.Square).then_inc(sqh_done, 1)
                if jj is not None:
                    attend(jj, 0, pt=True)
                if j is not None:
                    hi(a + 4)
                if forget:
                    forget()
                if jj is not None:
                    attend(jj, 1, exp=True)
                if j is not None:
                    hi(a + 5)
                    for t in range(2):
                        act.wait_ge(hs_mm, j * 2 + 2)
                        own.add(act.activation(sq[:, t, :], HS_BANK[t][:, :], ACT.Ln, bias=eps[:, 0:1]))
                    own.settle()
                    for t, dst in enumerate((s_b, s_c)):
                        act.activation(dst[:, :], sq[:, t, :], ACT.Exp, scale=-0.5).then_inc(hr_done, 1)

            def fox():
                act.wait_ge(wf_in, 32)
                act.activation(wf_hi[:, :, :], wf_raw[:, :, :], ACT.Copy).then_inc(wf_split, 1)
                def forget():
                    act.wait_ge(z_ready, 1)
                    lz = cums[0:HEADS, :]
                    own.add(act.activation(lz, s_p[0:HEADS, :], ACT.Abs))
                    own.settle()
                    own.add(act.activation(lz, lz, ACT.Exp, scale=-1.0))
                    own.settle()
                    act.activation(lz, lz, ACT.Ln, bias=1.0).then_inc(f_act, 1)
                fox_step(At(S_FOX), 0, None, None, forget)
                fox_step(At(S_FOX + 4), 1, 0, None)
                with act.Fori(1, KT - 1) as i:
                    own.enter(i, 2, 1)
                    fox_step(At(S_FOX + 4, i, 4), i + 1, i, i - 1)
                    own.leave(KT - 1)
                fox_step(None, None, KT - 1, KT - 2)
                fox_step(None, None, None, KT - 1)
                steps(act, S_FOXO, KT, 2, down(2, S_FOXO)[1])

            def s5_small_functions():
                act.wait_ge(s5_small, 64)
                act.activation(s5s[:, 3, :], s5s[:, 2, :], ACT.Exp).then_inc(s5_act, 1)
                act.wait_ge(s5_par, 1)
                act.activation(s5s[:, 6, :], s5s[:, 4, :], ACT.Exp).then_inc(s5_act, 1)
                act.wait_ge(s5_par, 2)
                act.activation(s5s[:, 9, :], s5s[:, 7, :], ACT.Sin).then_inc(s5_act, 1)
                act.activation(s5s[:, 10, :], s5s[:, 8, :], ACT.Sin).then_inc(s5_act, 1)

            def s5():
                def in_step(i, p, a):
                    hi(a + 2)
                    if not isinstance(i, int) or i >= 2:
                        act.wait_ge(blk_mm, i - 1)
                    u_back(act, i, p, range(BLK // 2, BLK))
                by_tile(act, 2, S_S5I, in_step)

                def out_step(i, p, a):
                    act.wait_ge(rec_done, 1)
                    if not isinstance(i, int) or i >= 2:
                        act.wait_ge(out_mm, i - 1)
                    src = xs[:, :, :].rearrange("p j (t i r) -> p t i r j", t=2, r=4)
                    for t in range(2):
                        act.activation(sq[:, p, 4 * NBLK * t:4 * NBLK * (t + 1)].rearrange("p (r j) -> p r j", r=4),
                                       src[:, t, i, :, :], ACT.Copy).then_inc(xc_done, 1)
                    if not isinstance(i, int) or i >= 2:
                        y_back(act, i - 2, p, range(4, 8))
                    if not isinstance(i, int) or i >= 4:
                        gelu(i - 4, p)

                def gelu(i, p):
                    act.wait_ge(pre_gelu, i + 1)
                    act.activation(y[:, i, :], [s_p, lnr][p][:, :], ACT.Gelu_apprx_tanh).then_inc(gelu_done, 1)
                by_tile(act, 4, 0, out_step)
                gelu(KT - 4, 0)
                y_back(act, KT - 2, 0, range(4, 8))
                gelu(KT - 3, 1)
                y_back(act, KT - 1, 1, range(4, 8))
                gelu(KT - 2, 0)
                gelu(KT - 1, 1)

                def glu(a, j):
                    for s in range(2):
                        hi(a + (s + 2))
                        act.wait_ge(slot_mm, (a + s).n + 1)
                        wait(act, z_done, j * 2)
                        act.activation([s_b, s_c][s][:, :], bank[s][:, :], ACT.Sigmoid).then_inc(bank_free[s], 1)
                steps(act, S_GLU, KT, 2, glu, lead=1)
                steps(act, S_S5O, KT, 2, down(4, S_S5O)[1])

            act.wait_ge(x_in, 16)
            for k in range(KT):
                squares_x(0, k)
            act.wait_ge(c_in, 16)
            act.activation(csil[:, :], csil[:, :], ACT.Silu).then_inc(csil_done, 1)
            act.wait_ge(consts, 1)
            act.wait_ge(stat_x, KT)
            rsqrt(r_pre, PRE_BANK, rpre_done)
            hi(At(0))
            hi(At(1))
            act.wait_ge(mods_done, 1)
            for k in range(KT):
                act.wait_ge(xm_done, k + 1)
                wait(act, h_done, k - 1)
                for src, dst in ((xm[:, k, :], tmp), (xn[:, k, PAD:PAD + T], sq)):
                    act.activation(dst[:, k % 2, :], src, ACT.Identity, scale=amp1[:, k:k + 1],
                                   bias=mods[:, SH1 + k:SH1 + k + 1]).then_inc(mix_mod, 1)
            s5_small_functions()
            for m in range(KT):
                if m % 4 == 0:
                    hi(At(S_POOL + m // 4 + 2))
                act.wait_ge(x_pool, m + 1)
                wait(act, acc_add, m - 1)
                act.activation(sq[:, m % 2, :], y[:, m, :], ACT.Square).then_inc(sq_done, 1)
            boundary(0)
            ffn(1, S_UP1A, conv_up, 0)
            boundary(1)
            fox()
            boundary(2)
            ffn(3, S_UP2A, silu_up, 2 * HH)
            boundary(3)
            s5()
            boundary(4)
            ffn(5, S_UP3A, silu_up, 4 * HH)
            boundary(5)

        @block.vector
        def _(dve):
            own = Tally(dve, dve_own)

            def lo(a):
                if a.n0 >= SLOTS:
                    return
                width = slot_width(a.n0)
                dve.wait_ge(hi_done, a.n + 1)
                dve.tensor_tensor(w_lo[:, a.s, 0:width], raw[:, a.s, 0:width],
                                  w_hi[:, a.s, 0:width].bitcast(F32), ALU.subtract).then_inc(lo_done, 1)

            def split(src, dst_hi, dst_lo, done):
                own.settle()
                own.add(dve.tensor_copy(dst_hi, src))
                own.settle()
                dve.tensor_tensor(dst_lo, src, dst_hi.bitcast(F32), ALU.subtract).then_inc(done, 1)

            def add_square(q, m, k2):
                dve.wait_ge(sq_done, m + (KT + 2 * KT * q + 1))
                own.settle()
                own.add(dve.tensor_tensor(acc[:, :], acc[:, :], sq[:, k2, :], ALU.add))
                own.settle()
                dve.sem_inc(acc_add, 1)

            def boundary(q):
                dve.wait_ge(rpost_done, q + 1)
                for k in range(KT + 1):
                    if k < KT:
                        own.add(dve.scalar_tensor_tensor(tmp[:, k % 2, :], y[:, k, :], POST[q](k),
                                                         r_post[:, :], ALU.mult, ALU.mult))
                        own.settle()
                        dve.tensor_tensor(x[:, k, :], x[:, k, :], tmp[:, k % 2, :], ALU.add).then_inc(x_upd, 1)
                    if k and q < len(PRE) and PRE[q]:
                        dve.wait_ge(hh_done, hh_before[q] + k)
                        dve.scalar_tensor_tensor(hl[:, k - 1, :], x[:, k - 1, :], PRE[q](k - 1),
                                                 hh[:, k - 1, :].bitcast(F32), ALU.mult,
                                                 ALU.subtract).then_inc(h_done, 1)
                if q == 0:
                    dve.wait_ge(rpre_done, 2)
                    for k in range(KT):
                        own.add(dve.scalar_tensor_tensor(tmp[:, k % 2, :], x[:, k, :], amp2[:, k:k + 1],
                                                         r_pre[:, :], ALU.mult, ALU.mult))
                        own.settle()
                        own.add(dve.tensor_scalar(s_a[:, :], tmp[:, k % 2, :], mods[:, SH2 + k:SH2 + k + 1], None,
                                                  ALU.add))
                        split(s_a[:, :], hh[:, k, :], hl[:, k, :], h_done)

            def down(q):
                def first_half(a, j):
                    for s in range(2):
                        lo(a + (s + 2))
                        dve.wait_ge(slot_mm, (a + s).n + 1)
                        dve.tensor_copy(y[:, j * 2 + s, :], bank[s][:, :]).then_inc(bank_free[s], 1)

                def second_half(a, j):
                    for s in range(2):
                        lo(a + (s + 2))
                        dve.wait_ge(slot_mm, (a + s).n + 1)
                        m = j * 2 + s
                        dve.tensor_tensor(y[:, m, :], y[:, m, :], bank[s][:, :], ALU.add).then_inc(bank_free[s], 1)
                        add_square(q, m, s)
                return first_half, second_half

            def conv_up(half, base):
                def body(a, j):
                    i = j + half * HH
                    for s in range(2):
                        lo(a + (s + 2))
                        c = [s_a, s_c][s]
                        b = bank[s]
                        dve.wait_ge(conv_mid, (j + base) * 2 + s + 1)
                        own.add(dve.scalar_tensor_tensor(c[:, 1:T], b[:, 0:T - 1], convw[:, i, 4 * s:4 * s + 1],
                                                         c[:, 1:T], ALU.mult, ALU.add))
                        own.settle()
                        dve.scalar_tensor_tensor(c[:, 0:T - 1], b[:, 1:T], convw[:, i, 4 * s + 2:4 * s + 3],
                                                 c[:, 0:T - 1], ALU.mult, ALU.add).then_inc(bank_free[s], 1)
                    dve.wait_ge(act_done, j + base + 1)
                    dve.wait_ge(bank_free[1], (a + 1).turns + 1)
                    own.add(dve.tensor_tensor(s_p[:, :], s_b[:, :], s_c[:, :], ALU.mult))
                    split(s_p[:, :], hid_hi[:, j, :], hid_lo[:, j, :], hid_done)
                return body, 4

            def silu_up(half, base):
                def body(a, j):
                    lo(a + 2)
                    dve.wait_ge(slot_mm, a.n + 1)
                    dve.tensor_tensor(s_a[:, :], bank[0][:, :], r_pre[:, :], ALU.mult).then_inc(bank_free[0], 1)
                    lo(a + 3)
                    dve.wait_ge(act_done, j + base + 1)
                    own.add(dve.tensor_tensor(s_c[:, :], s_b[:, :], r_pre[:, :], ALU.mult))
                    own.settle()
                    dve.wait_ge(slot_mm, a.n + 2)
                    dve.tensor_tensor(s_p[:, :], s_c[:, :], bank[1][:, :], ALU.mult).then_inc(bank_free[1], 1)
                    dve.wait_ge(bank_free[1], (a + 1).turns + 1)
                    split(s_p[:, :], hid_hi[:, j, :], hid_lo[:, j, :], hid_done)
                return body, 2

            def ffn(q, first, up, base):
                lo_half, hi_half = down(q)
                dve.wait_ge(rpre_done, q + 1)
                body, adds = up(0, base)
                steps(dve, first, 2 * HH, 2, body, own, adds)
                if q == 1:
                    dve.wait_ge(csil_done, 2)
                    for b in range(3):
                        dve.wait_ge(g2_in[b], 16)
                        two_dots(g2_w[:, b, :], g2_csil, b, g2_used)
                steps(dve, first + 2 * HH, KT, 2, lo_half)
                if q == 1:
                    dve.wait_ge(g2_in[3], 16)
                    two_dots(g2_w[:, 0, :], g2_csil, 3, g2_used)
                body, adds = up(1, base + HH)
                steps(dve, first + 2 * HH + KT, 2 * HH, 2, body, own, adds)
                own.add(dve.memset(acc[:, :], 0.0))
                steps(dve, first + 4 * HH + KT, KT, 2, hi_half, own, 2)

            def mixer_out(q):
                def body(a, j):
                    for s in range(2):
                        lo(a + (s + 2))
                        dve.wait_ge(slot_mm, (a + s).n + 1)
                        m = j * 2 + s
                        dve.tensor_copy(y[:, m, :], bank[s][:, :]).then_inc(bank_free[s], 1)
                        add_square(q, m, s)
                return body

            def select_c(jj, head):
                hd = jj * 2 + head
                wait(dve, s_mm, hd)
                for t, src in enumerate((c_hi, c_lo)):
                    dve.tensor_scalar(dsel[0:HEADS, t, :], src[0:HEADS, :].bitcast(F32), head_col(jj, head),
                                      None, ALU.mult).then_inc(dsel_done, 1)

            def head_col(jj, head):
                return ident[0:HEADS, 0:HEADS].rearrange("p (j h) -> p j h", h=2)[:, jj, head:head + 1]

            def softmax(jj, head):
                hd = jj * 2 + head
                dve.wait_ge(s_mm, hd + 1)
                for qb in range(QB):
                    own.add(dve.tensor_reduce(rinv[:, qb:qb + 1], S_AT[qb], mybir.AxisListType.X, ALU.max))
                own.settle()
                dve.tensor_scalar(nmax[:, :], rinv[:, :], -1.0, None, ALU.mult).then_inc(mx_done, 1)
                dve.wait_ge(exp_done, hd + 1)
                own.add(dve.reciprocal(rinv[:, :], rsum[:, :]))
                own.settle()
                for qb in range(QB):
                    pr = prob[:, P_AT[qb]:P_AT[qb] + P * (qb + 1)]
                    p = dve.tensor_scalar(pr, pr, rinv[:, qb:qb + 1], None, ALU.mult)
                p.then_inc(p_done, 1)

            def pt_split(jj, head):
                hd = jj * 2 + head
                for t, (b, c, w) in enumerate(T_PARTS):
                    dve.wait_ge(pth_done, hd * 3 + (t + 1))
                    dve.tensor_tensor(pt_lo[:, c:c + w], b, pt_hi[:, c:c + w].bitcast(F32), ALU.subtract)\
                       .then_inc(pt_done, 1)

            def head_out(jj, head):
                r = slice(HD * head, HD * head + HD)
                dve.wait_ge(pv_mm, jj * 2 + (head + 1))
                dve.wait_ge(g_done, jj + 1)
                own.add(dve.tensor_tensor(s_p[r, :], PV_BANK[r, :], gsig[r, :], ALU.mult))
                split(s_p[r, :], hid_hi[r, jj, :], hid_lo[r, jj, :], o_done)

            def fox_step(a, j, jj, kk, forget=None):
                if jj is not None:
                    select_c(jj, 0)
                if j is not None:
                    lo(a + 2)
                    dve.wait_ge(slot_mm, a.n + 1)
                    dve.tensor_tensor(qf[:, 0, :], bank[0][:, :], r_pre[:, :], ALU.mult).then_inc(bank_free[0], 1)
                if kk is not None:
                    head_out(kk, 1)
                if jj is not None:
                    dve.wait_ge(vh_done, jj + 1)
                    flat = "p a b -> p (a b)"
                    dve.tensor_tensor(v_lo[:, :, :].rearrange(flat), V_BANK[:, :],
                                      v_hi[:, :, :].rearrange(flat).bitcast(F32), ALU.subtract).then_inc(v_done, 1)
                    softmax(jj, 0)
                    select_c(jj, 1)
                if j is not None:
                    lo(a + 3)
                    dve.wait_ge(slot_mm, a.n + 2)
                    dve.tensor_tensor(qf[:, 1, :], bank[1][:, :], r_pre[:, :], ALU.mult).then_inc(bank_free[1], 1)
                if jj is not None:
                    pt_split(jj, 0)
                if j is not None:
                    lo(a + 4)
                    dve.wait_ge(slot_mm, a.n + 3)
                    own.add(dve.tensor_tensor(vt[:, :], bank[0][:, :], r_pre[:, :], ALU.mult))
                    own.settle()
                    dve.sem_inc(bank_free[0], 1)
                    dve.sem_inc(vt_done, 1)
                if forget:
                    forget()
                if jj is not None:
                    head_out(jj, 0)
                    softmax(jj, 1)
                if j is not None:
                    lo(a + 5)
                    dve.wait_ge(slot_mm, a.n + 4)
                    if jj is not None:
                        dve.wait_ge(g_done, jj + 1)
                    dve.tensor_tensor(s_a[:, :], bank[1][:, :], r_pre[:, :], ALU.mult).then_inc(bank_free[1], 1)
                if jj is not None:
                    pt_split(jj, 1)
                if j is not None:
                    for t, hr in enumerate((s_b, s_c)):
                        dve.wait_ge(hr_done, j * 2 + (t + 1))
                        if jj is not None:
                            dve.wait_ge(s_mm, jj * 2 + 2)
                        own.add(dve.scalar_tensor_tensor(tmp[:, t, :], qf[:, t, :], qk_gain[:, t:t + 1], hr[:, :],
                                                         ALU.mult, ALU.mult))
                        split(tmp[:, t, :], qk[:, 2 * t, :], qk[:, 2 * t + 1, :], qk_done)

            def fox():
                own.add(dve.tensor_scalar(qk_gain[:, 0:1], vec[:, QK_GAIN:QK_GAIN + 1], HD ** -0.5, None, ALU.mult))
                own.add(dve.tensor_copy(qk_gain[:, 1:2], vec[:, QK_GAIN + 1:QK_GAIN + 2]))
                own.add(dve.memset(dsel[:, :, :].bitcast(mybir.dt.uint32), 0))
                dve.wait_ge(wf_split, 1)
                dve.tensor_tensor(wf_lo[:, :, :], wf_raw[:, :, :], wf_hi[:, :, :].bitcast(F32), ALU.subtract)\
                   .then_inc(wf_split, 1)
                dve.wait_ge(rpre_done, 3)
                def forget():
                    dve.wait_ge(f_mm, 1)
                    z, lf, one = s_p[0:HEADS, :], tmp[0:HEADS, 1, :], tmp[0:HEADS, 0, :]
                    own.add(dve.tensor_tensor(lf, bank[5][0:HEADS, :], r_pre[0:HEADS, :], ALU.mult))
                    own.settle()
                    own.add(dve.tensor_scalar(z, lf, bf_col[0:HEADS, 0:1], None, ALU.add))
                    own.settle()
                    dve.sem_inc(z_ready, 1)
                    own.add(dve.tensor_scalar(lf, z, 0.0, None, ALU.min))
                    own.add(dve.memset(one, 1.0))
                    own.settle()
                    dve.wait_ge(f_act, 1)
                    own.add(dve.tensor_tensor(lf, lf, cums[0:HEADS, :], ALU.subtract))
                    own.settle()
                    own.add(dve.tensor_tensor_scan(cums[0:HEADS, :], one, lf, 0.0, ALU.mult, ALU.add))
                    own.settle()
                    own.add(dve.tensor_scalar(z, cums[0:HEADS, :], -1.0, None, ALU.mult))
                    own.settle()
                    own.add(dve.tensor_copy(c_hi[0:HEADS, :], z))
                    own.settle()
                    own.add(dve.tensor_tensor(c_lo[0:HEADS, :], z, c_hi[0:HEADS, :].bitcast(F32), ALU.subtract))
                    own.settle()
                fox_step(At(S_FOX), 0, None, None, forget)
                fox_step(At(S_FOX + 4), 1, 0, None)
                with dve.Fori(1, KT - 1) as i:
                    own.enter(i, FOX_ADDS, 1)
                    fox_step(At(S_FOX + 4, i, 4), i + 1, i, i - 1)
                    own.leave(KT - 1)
                fox_step(None, None, KT - 1, KT - 2)
                fox_step(None, None, None, KT - 1)
                own.add(dve.memset(acc[:, :], 0.0))
                steps(dve, S_FOXO, KT, 2, mixer_out(2), own, 2)

            def tt(out_, a, b, op):
                own.add(dve.tensor_tensor(out_, a, b, op))
                own.settle()

            def ts(out_, a, s1, s2, op0, op1=None):
                own.add(dve.tensor_scalar(out_, a, s1, s2, op0) if op1 is None else
                        dve.tensor_scalar(out_, a, s1, s2, op0, op1))
                own.settle()

            def two_dots(w, c, b, used):
                for t in range(2):
                    wt = w[:, t * D:(t + 1) * D]
                    dot = dve.tensor_tensor_reduce(wt, wt, c[:, :], 1.0, 0.0, ALU.mult, ALU.add,
                                                   accum_out=dots[:, 2 * b + t:2 * b + t + 1])
                dot.then_inc(used, 1)

            def add_bias(i):
                six = "p (i k) -> p i k"
                own.add(dve.tensor_tensor(mods[:, :].rearrange(six, k=KT)[:, i, :], dots[:, :],
                                          vec[:, ADA_B:ADA_B + 6 * KT].rearrange(six, k=KT)[:, i, :], ALU.add))
                own.settle()

            def modulation(i):
                for b in range(4):
                    dve.wait_ge(ada_full[b], (i + 1) * 16)
                    two_dots(ada_w[:, b, :], csil, b, ada_used)
                dve.wait_ge(ada_used, (i + 1) * 4)
                add_bias(i)

            def scaled(dst, first, name, plus):
                own.add(dve.scalar_tensor_tensor(dst[:, :], mods[:, first:first + KT], plus,
                                                 vec[:, VCOL[name]:VCOL[name] + KT], ALU.add, ALU.mult))

            def s5():
                by_block = "p (j s) -> p s j"
                dve.wait_ge(rpre_done, 5)
                dve.wait_ge(s5_par, 3)

                def blocks_out(i):
                    dve.wait_ge(blk_mm, i + 1)
                    dst = xs[:, :, :].rearrange("p j (t i r) -> p t i r j", t=2, r=4)
                    for t in range(2):
                        dve.tensor_copy(dst[:, t, i, :, :],
                                        bank[6][:, 4 * NBLK * t:4 * NBLK * (t + 1)].rearrange("p (r j) -> p r j", r=4))\
                           .then_inc(blk_done, 1)
                    dve.tensor_copy(yb[:, i, :], bank[7][:, :]).then_inc(blk_done, 1)

                def in_step(i, p, a):
                    dve.wait_ge(slot_mm, a.n + 1)
                    dve.tensor_tensor(y[:, i, :].rearrange("p (s j) -> p s j", s=BLK),
                                      bank[p][:, :].rearrange(by_block, s=BLK),
                                      r_pre[:, :].rearrange(by_block, s=BLK), ALU.mult).then_inc(bank_free[p], 1)
                    lo(a + 2)
                    if not isinstance(i, int) or i:
                        blocks_out(i - 1)
                by_tile(dve, 1, S_S5I, in_step)
                blocks_out(KT - 1)

                def fac(e, part):
                    return factors[:, e, part, :]
                tt(fac(0, 0), pw_re[:, :, BLK], ones_row, ALU.mult)
                tt(fac(0, 1), pwn_im[:, :, BLK], ones_row, ALU.mult)
                tt(fac(0, 2), pw_im[:, :, BLK], ones_row, ALU.mult)
                for e in range(1, LEVELS + 1):
                    before = fac(e - 1, 0), fac(e - 1, 2)
                    tt(fac(e, 0), before[0], before[0], ALU.mult)
                    tt(fac(e, 1), before[1], before[1], ALU.mult)
                    tt(fac(e, 0), fac(e, 0), fac(e, 1), ALU.subtract)
                    tt(fac(e, 2), before[0], before[1], ALU.mult)
                    ts(fac(e, 1), fac(e, 2), -2.0, None, ALU.mult)
                    ts(fac(e, 2), fac(e, 2), 2.0, None, ALU.mult)

                def mac(first, step, n, e):
                    def rows(j):
                        return xs[:, :, :].rearrange("p (a b) c -> p a b c", b=step)[:, j // step:j // step + n, j % step, :]\
                            .rearrange("p a (t r) -> p a t r", t=2)
                    now, before = rows(first), rows(first - 2 ** e)
                    real = terms[:, 0, 0:n, :].rearrange("p a (t r) -> p a t r", t=2)
                    cross = terms[:, 1, 0:n, :].rearrange("p a (t r) -> p a t r", t=2)
                    for t in range(2):
                        f = fac(e, 0).unsqueeze(1).to_broadcast([P, n, PAIRS])
                        own.add(dve.tensor_tensor(real[:, :, t, :], f, before[:, :, t, :], ALU.mult))
                        f = fac(e, 1 + t).unsqueeze(1).to_broadcast([P, n, PAIRS])
                        own.add(dve.tensor_tensor(cross[:, :, t, :], f, before[:, :, 1 - t, :], ALU.mult))
                    own.settle()
                    own.add(dve.tensor_tensor(real, real, cross, ALU.add))
                    own.settle()
                    own.add(dve.tensor_tensor(now, now, real, ALU.add))
                    own.settle()

                dve.wait_ge(blk_done, 3 * KT)
                for e in range(LEVELS):
                    mac(2 ** (e + 1) - 1, 2 ** (e + 1), NBLK >> (e + 1), e)
                top_step = 2 ** LEVELS
                for j in range(2 * top_step - 1, NBLK, top_step):
                    mac(j, top_step, 1, LEVELS)
                for e in reversed(range(LEVELS)):
                    mac(3 * 2 ** e - 1, 2 ** (e + 1), (NBLK >> (e + 1)) - 1, e)
                own.settle()
                dve.sem_inc(rec_done, 1)

                def pre(i, p):
                    dve.wait_ge(yt_in[p], (i - p) * 64 + 128)
                    if not isinstance(i, int) or i >= 2:
                        dve.wait_ge(gelu_done, i - 1)
                    dve.scalar_tensor_tensor([s_p, lnr][p][:, :], y[:, i, :], s5_d_col(i), tmp[:, p, :],
                                             ALU.mult, ALU.add).then_inc(pre_gelu, 1)

                def s5_d_col(i):
                    return vec[:, VCOL["s5_d"]:VCOL["s5_d"] + KT].rearrange("p (k o) -> p k o", o=1)[:, i, :]

                def post(i):
                    dve.wait_ge(gelu_done, i + 1)
                    own.add(dve.tensor_copy(hh[:, i, :], y[:, i, :]))
                    own.settle()
                    dve.tensor_tensor(hl[:, i, :], y[:, i, :], hh[:, i, :].bitcast(F32), ALU.subtract)\
                       .then_inc(h_done, 1)

                def out_step(i, p, a):
                    dve.wait_ge(out_mm, i + 1)
                    for h in range(2):
                        dst = yb[:, i, :].rearrange("p (g h j) -> p h g j", h=2, j=NBLK)[:, h, :, 1:NBLK]
                        add = dve.tensor_tensor(dst, dst, bank[4 + 2 * p + h][:, 0:4 * NBLK].rearrange(
                            "p (g j) -> p g j", g=4)[:, :, 0:NBLK - 1], ALU.add)
                    add.then_inc(yb_done, 1)
                    if not isinstance(i, int) or i >= 3:
                        pre(i - 3, 1 - p)
                    if not isinstance(i, int) or i >= 5:
                        post(i - 5)
                by_tile(dve, 6, 0, out_step, own, 1)
                for i in range(KT - 3, KT):
                    pre(i, i % 2)
                    post(i - 2)
                post(KT - 2)
                post(KT - 1)

                def glu(a, j):
                    for s in range(2):
                        m = j * 2 + s
                        lo(a + (s + 2))
                        dve.wait_ge(bank_free[s], (a + s).turns + 1)
                        z = [s_b, s_c][s][:, :]
                        own.add(dve.tensor_tensor(z, z, y[:, m, :], ALU.mult))
                        split(z, hid_hi[:, m, :], hid_lo[:, m, :], z_done)
                steps(dve, S_GLU, KT, 2, glu, own, 4)
                own.add(dve.memset(acc[:, :], 0.0))

                def s5_out(a, j):
                    for s in range(2):
                        lo(a + (s + 2))
                        dve.wait_ge(slot_mm, (a + s).n + 1)
                        m = j * 2 + s
                        dve.tensor_copy(y[:, m, :].rearrange("p (j s) -> p j s", s=BLK),
                                        bank[s][:, :].rearrange("p (s j) -> p j s", s=BLK)).then_inc(bank_free[s], 1)
                        add_square(4, m, s)
                steps(dve, S_S5O, KT, 2, s5_out, own, 2)

            FOX_ADDS = 2 * (QB + 1) + 2 * 2 + 1 + 2 * 2
            hh_before = [0, 0, KT, 2 * KT, 3 * KT]
            own.add(dve.memset(eps[:, :], EPS))
            own.add(dve.memset(mean[:, :], 1.0 / D))
            own.add(dve.memset(acc[:, :], 0.0))
            own.add(dve.memset(ones_f[:, :], 1.0))
            own.settle()
            own.add(dve.tensor_copy(ones_r[:, :], ones_f[:, :]))
            own.add(dve.memset(blk64[:, :], 0.0))
            own.settle()
            for h in range(2):
                own.add(dve.memset(blk64[HD * h:HD * h + HD, HD * h:HD * h + HD], 1.0 / HD))
            own.settle()
            dve.sem_inc(consts, 1)
            dve.wait_ge(s5_small, 64)
            v = lambda k: s5s[:, k, :]
            tt(v(16), v(0), v(0), ALU.mult)
            tt(v(17), v(1), v(1), ALU.mult)
            tt(v(15), v(16), v(17), ALU.add)
            dve.reciprocal(v(14), v(15)).then_inc(s5_den, 1)
            dve.wait_ge(small_in, 32)
            dve.wait_ge(csil_done, 1)
            with dve.Fori(0, 2) as i:
                own.enter(i, 1)
                modulation(i)
                own.leave(2)
            scaled(amp1, SC1, "mix_pre_g", 1.0)
            own.settle()
            dve.sem_inc(mods_done, 1)

            def mixer_input(tiles):
                for k in tiles:
                    dve.wait_ge(mix_mod, 2 * k + 2)
                    wait(dve, h_done, k)
                    own.add(dve.tensor_tensor(s_a[:, :], tmp[:, k % 2, :], sq[:, k % 2, :], ALU.subtract))
                    split(s_a[:, :], hh[:, k, :], hl[:, k, :], h_done)

            modulation(2)
            scaled(gpost1, G1, "mix_post_g", 0.0)
            mixer_input(range(KT // 2))
            modulation(3)
            mixer_input(range(KT // 2, KT))
            lo(At(0))
            lo(At(1))
            modulation(4)
            scaled(amp2, SC2, "ffn_pre_g", 1.0)
            own.settle()
            for m in range(KT):
                s = m // 4
                if m % 4 == 0:
                    lo(At(S_POOL + s + 2))
                    dve.wait_ge(slot_mm, S_POOL + s + 1)
                own.settle()
                own.add(dve.tensor_scalar(y[:, m, :], bank[POOL_BANKS[m]][:, :], col("pool_scale", m), None, ALU.mult))
                own.settle()
                dve.sem_inc(x_pool, 1)
                if m % 4 == 3:
                    dve.sem_inc(bank_free[s], 1)
                if m:
                    add_square(0, m - 1, (m - 1) % 2)
            add_square(0, KT - 1, (KT - 1) % 2)
            boundary(0)
            ffn(1, S_UP1A, conv_up, 0)
            dve.wait_ge(g2_used, 4)
            add_bias(5)
            scaled(gpost2, G2, "ffn_post_g", 0.0)
            own.add(dve.memset(wf_raw[:, :, :], 0.0))
            own.settle()
            dve.sem_inc(wf_zero, 1)
            boundary(1)
            fox()
            boundary(2)
            ffn(3, S_UP2A, silu_up, 2 * HH)
            boundary(3)
            s5()
            boundary(4)
            ffn(5, S_UP3A, silu_up, 4 * HH)
            boundary(5)

        @block.gpsimd
        def _(pool):
            pool.memset(ident[:, :], 0.0).then_inc(ident_own, 1)
            pool.wait_ge(ident_own, 1)
            pool.affine_select(out=ident[:, :], in_=ident[:, :], compare_op=ALU.not_equal, fill=1.0, base=0,
                               pattern=[[-1, P]], channel_multiplier=1).then_inc(ident_own, 1)
            pool.memset(causal[:, :], 0.0).then_inc(ident_own, 1)
            pool.wait_ge(ident_own, 3)
            pool.tensor_copy(ident_bf[:, :], ident[:, :]).then_inc(ident_own, 1)
            pool.affine_select(out=causal[:, :], in_=causal[:, :], compare_op=ALU.is_ge, fill=NEG, base=0,
                               pattern=[[-1, P]], channel_multiplier=1).then_inc(ident_own, 1)
            pool.wait_ge(ident_own, 5)
            pool.sem_inc(ident_done, 1)
            own = Tally(pool, pool_own)
            SH = [P, 4, BLK, CH]

            def tt(out_, a, b, op):
                own.add(pool.tensor_tensor(out_, a, b, op))
                own.settle()

            def ts(out_, a, s1, s2, op0, op1=None):
                own.add(pool.tensor_scalar(out_, a, s1, s2, op0) if op1 is None else
                        pool.tensor_scalar(out_, a, s1, s2, op0, op1))
                own.settle()

            own.add(pool.memset(xn[:, :, :], 0.0))
            pool.wait_ge(rcnt_in, 16)
            pool.wait_ge(rpre_done, 1)
            own.settle()
            for k in range(KT):
                g = k // 2
                w = WINDOWS[g]
                tt(xn[:, k, PAD:PAD + T], x[:, k, :], r_pre[:, :], ALU.mult)
                src, n, span, b = xn[:, k, :], PW, 1, 0
                while span < w:
                    n -= span
                    tt(pool_s[:, b, 0:n], src[:, 0:n], src[:, span:span + n], ALU.add)
                    src, span, b = pool_s[:, b, :], 2 * span, 1 - b
                at0 = PAD - w // 2
                tt(xm[:, k, :], src[:, at0:at0 + T], rcnt[:, g, :], ALU.mult)
                pool.sem_inc(xm_done, 1)

            def s5_parameters():
                v = lambda k: s5s[:, k, :]
                lam_re, lam_im, dt = v(0), v(1), v(3)
                pool.wait_ge(s5_act, 1)
                tt(v(4), lam_re, dt, ALU.mult)
                pool.sem_inc(s5_par, 1)
                tt(v(5), lam_im, dt, ALU.mult)
                ts(v(11), v(5), 1.0 / TWO_PI, None, ALU.mult)
                ts(v(11), v(11), ROUND, None, ALU.add)
                ts(v(11), v(11), -ROUND, None, ALU.add)
                for part in TWO_PI_PARTS:
                    ts(v(12), v(11), part, None, ALU.mult)
                    tt(v(5), v(5), v(12), ALU.subtract)
                ts(v(7), v(5), PI_BELOW, -PI_BELOW, ALU.min, ALU.max)
                ts(v(12), v(7), 0.0, None, ALU.max)
                ts(v(13), v(7), 0.0, None, ALU.min)
                tt(v(12), v(12), v(13), ALU.subtract)
                ts(v(8), v(12), -1.0, float(np.pi / 2), ALU.mult, ALU.add)
                pool.sem_inc(s5_par, 1)
                pool.wait_ge(s5_act, 4)
                own.add(pool.memset(pw_re[:, :, 0:1], 1.0))
                own.add(pool.memset(pw_im[:, :, 0:1], 0.0))
                tt(pw_re[:, :, 1], v(6), v(10), ALU.mult)
                tt(pw_im[:, :, 1], v(6), v(9), ALU.mult)

                def power(dst, src, mul):
                    n = dst.stop - dst.start
                    m_re = pw_re[:, :, mul:mul + 1].to_broadcast([P, PAIRS, n])
                    m_im = pw_im[:, :, mul:mul + 1].to_broadcast([P, PAIRS, n])
                    t1 = pool_s[:, 0, 0:PAIRS * n].rearrange("p (a b) -> p a b", b=n)
                    t2 = pool_s[:, 1, 0:PAIRS * n].rearrange("p (a b) -> p a b", b=n)
                    tt(t1, pw_re[:, :, src], m_re, ALU.mult)
                    tt(t2, pw_im[:, :, src], m_im, ALU.mult)
                    tt(pw_re[:, :, dst], t1, t2, ALU.subtract)
                    tt(t1, pw_re[:, :, src], m_im, ALU.mult)
                    tt(t2, pw_im[:, :, src], m_re, ALU.mult)
                    tt(pw_im[:, :, dst], t1, t2, ALU.add)
                power(slice(2, 3), slice(1, 2), 1)
                power(slice(3, 5), slice(1, 3), 2)
                power(slice(5, 9), slice(1, 5), 4)
                ts(pwn_im[:, :, :], pw_im[:, :, :], -1.0, None, ALU.mult)
                ts(v(11), pw_re[:, :, 1], -1.0, None, ALU.add)
                pool.wait_ge(s5_den, 1)
                a_im = pw_im[:, :, 1]
                tt(v(12), v(11), lam_re, ALU.mult)
                tt(v(13), a_im, lam_im, ALU.mult)
                tt(v(12), v(12), v(13), ALU.add)
                tt(z_re[:, :], v(12), v(14), ALU.mult)
                tt(v(12), a_im, lam_re, ALU.mult)
                tt(v(13), v(11), lam_im, ALU.mult)
                tt(v(12), v(12), v(13), ALU.subtract)
                tt(z_im[:, :], v(12), v(14), ALU.mult)
                pool.sem_inc(s5_par, 1)
            s5_parameters()

            def product(out_, p1, m1, p2, m2, op, shape):
                view = out_.rearrange("p r (s c) -> p r s c", c=CH)
                t = prod[:, :, 0:shape[2] * CH].rearrange("p r (s c) -> p r s c", c=CH)
                own.add(pool.tensor_tensor(view, p1, m1, ALU.mult))
                own.add(pool.tensor_tensor(t, p2, m2, ALU.mult))
                own.settle()
                own.add(pool.tensor_tensor(view, view, t, op))
                own.settle()

            def powers(t, i, n):
                return t[:, 4 * i:4 * i + 4, 0:n].unsqueeze(3).to_broadcast([P, 4, n, CH])

            def matrix(t, part, i, n):
                return t[:, part, 4 * i:4 * i + 4, :].unsqueeze(2).to_broadcast([P, 4, n, CH])

            pool.wait_ge(stat_y, 3)
            own.add(pool.memset(kt[:, :, :], 0.0))
            own.settle()
            pool.sem_inc(zeros_done, 1)
            pool.wait_ge(s5_big, 32)
            zr = z_re[:, :].unsqueeze(2).to_broadcast([P, PAIRS, CH])
            zi = z_im[:, :].unsqueeze(2).to_broadcast([P, PAIRS, CH])
            t1 = prod_b[:, :, :]
            for part, other, op in ((0, 1, ALU.subtract), (1, 0, ALU.add)):
                tt(bt[:, part, :, :], zr, b_raw[:, part, :, :], ALU.mult)
                tt(t1, zi, b_raw[:, other, :, :], ALU.mult)
                tt(bt[:, part, :, :], bt[:, part, :, :], t1, op)

            for i in range(KT):
                wait(pool, k_mm, i)
                n, shape = BLK, [P, 4, BLK, CH]
                product(r_tab[:, 0, :, :], powers(pw_re, i, n), matrix(bt, 0, i, n), powers(pw_im, i, n),
                        matrix(bt, 1, i, n), ALU.subtract, shape)
                product(r_tab[:, 1, :, :], powers(pw_re, i, n), matrix(bt, 1, i, n), powers(pw_im, i, n),
                        matrix(bt, 0, i, n), ALU.add, shape)
                for t in range(2):
                    own.add(pool.tensor_copy(btc[:, t, :, :], bt[:, t, 4 * i:4 * i + 4, :]))
                own.settle()
                pool.sem_inc(r_done, 1)
                wait(pool, q_out, i * 16)
                n, shape = NPW, [P, 4, NPW, CH]
                product(q_tab[:, 0, :, :], powers(pw_re, i, n), matrix(cc, 0, i, n), powers(pw_im, i, n),
                        matrix(cc, 1, i, n), ALU.subtract, shape)
                product(q_tab[:, 1, :, :], powers(pwn_im, i, n), matrix(cc, 0, i, n), powers(pw_re, i, n),
                        matrix(cc, 1, i, n), ALU.subtract, shape)
                pool.sem_inc(q_done, 1)

        @block.tensor
        def _(pe):
            def passes(dst, w_h, w_l, r_h, r_l, first, last):
                pe.matmul(dst, w_h, r_h, start=first, stop=False)
                pe.matmul(dst, w_h, r_l, start=False, stop=False)
                return pe.matmul(dst, w_l, r_h, start=False, stop=last)

            def slot(a, rh, rl, kts, before=None, first=0, end=None):
                if first == 0:
                    pe.wait_ge(lo_done, a.n + 1)
                    wait(pe, bank_free[a.s], a.turns)
                for k in range(first, kts if end is None else end):
                    if before:
                        before(k)
                    mm = passes(bank[a.s][:, :], w_hi[:, a.s, k * P:(k + 1) * P], w_lo[:, a.s, k * P:(k + 1) * P],
                                rh[:, k, :], rl[:, k, :], k == 0, k == kts - 1)
                if end is None:
                    mm.then_inc(slot_mm, 1)

            def stat(q, k):
                pe.wait_ge(sq_done, 2 * KT * q + k + 1)
                pe.matmul(bank[PRE_BANK][:, :], mean[:, :], sq[:, k % 2, :], start=k == 0,
                          stop=k == KT - 1, skip_group_check=True).then_inc(stat_x, 1)

            def boundary(q):
                pe.wait_ge(acc_add, KT * (q + 1))
                pe.matmul(bank[POST_BANK][:, :], mean[:, :], acc[:, :], start=True, stop=True).then_inc(stat_y, 1)
                if q == 0:
                    for k in range(KT):
                        stat(q + 1, k)

            def first_input(q):
                def before(k):
                    if PRE[q]:
                        stat(q + 1, k)
                    pe.wait_ge(h_done, KT * H_SET[q] + k + 1)
                return before

            def run(first, count, rh, rl, kts, before=None, after=None):
                start = 0
                if before:
                    slot(At(first), rh, rl, kts, before)
                    slot(At(first + 1), rh, rl, kts)
                    if after:
                        after(0)
                    start = 2
                with pe.Fori(0, (count - start) // 2) as i:
                    for s in range(2):
                        slot(At(first + start, i, 2) + s, rh, rl, kts)
                    if after:
                        after(i + start // 2)

            def hid_input(done):
                def before(k):
                    pe.wait_ge(hid_done, done + k + 1)
                return before

            def rows(g):
                return slice(STATE * (g % 2), STATE * (g % 2) + STATE)

            def make_tables(i):
                pe.wait_ge(r_done, i + 1)
                pe.wait_ge(q_done, i + 1)
                wait(pe, w1_done, i * 2)
                wait(pe, kt_done, i * 2)
                for t in range(2):
                    for r4 in range(4):
                        mm = pe.transpose(bank[4 + t][:, P * r4:P * r4 + P], r_tab[:, t, r4, :], ident[:, :])
                mm.then_inc(rt_mm, 1)
                for g in range(8):
                    dst = bank[6 + g % 2][0:CH, P * (g // 2):P * (g // 2) + P]
                    for t in range(2):
                        mm = pe.matmul(dst, btc[rows(g), t, g // 2, :], q_tab[rows(g), t, g // 2, 0:P],
                                       start=t == 0, stop=t == 1)
                mm.then_inc(k_mm, 1)

            def ffn(q, first, base, tables=False):
                run(first, 2 * HH, hh, hl, KT, first_input(q))
                run(first + 2 * HH, KT, hid_hi, hid_lo, HH, hid_input(base), make_tables if tables else None)
                run(first + 2 * HH + KT, 2 * HH, hh, hl, KT)
                run(first + 4 * HH + KT, KT, hid_hi, hid_lo, HH, hid_input(base + HH),
                    (lambda j: make_tables(j + KT // 2)) if tables else None)

            pe.wait_ge(consts, 1)
            for k in range(KT):
                stat(0, k)
            for s in range(2):
                pe.wait_ge(lo_done, S_POOL + s + 1)
                pe.wait_ge(h_done, 4 * (s + 1))
                for m in range(4):
                    g = m // 2
                    for k in range(2):
                        c = (g * 2 + k) * 2 * P + (m % 2) * P
                        mm = passes(bank[POOL_BANKS[4 * s + m]][:, :], w_hi[:, s, c:c + P], w_lo[:, s, c:c + P],
                                    hh[:, 4 * s + 2 * g + k, :], hl[:, 4 * s + 2 * g + k, :], k == 0, k == 1)
                mm.then_inc(slot_mm, 1)
            boundary(0)

            ffn(0, S_UP1A, 0)
            boundary(1)
            def scores(jj, head):
                hd = jj * 2 + head
                r = slice(HD * head, HD * head + HD)
                pe.wait_ge(qk_done, jj * 2 + 2)
                pe.wait_ge(dsel_done, hd * 2 + 2)
                if head:
                    pe.wait_ge(pt_done, hd * 3)
                for blocks in ((0, 1, 3), (2,)):
                    for qb in blocks:
                        w = P * (qb + 1)
                        dst, qs = S_AT[qb], slice(P * qb, P * qb + P)
                        pe.matmul(dst, qk[r, 0, qs], qk[r, 2, 0:w], start=True, stop=False)
                        pe.matmul(dst, qk[r, 0, qs], qk[r, 3, 0:w], start=False, stop=False)
                        pe.matmul(dst, qk[r, 1, qs], qk[r, 2, 0:w], start=False, stop=False)
                    for qb in blocks:
                        w = P * (qb + 1)
                        dst = S_AT[qb]
                        pe.matmul(dst[:, w - P:w], ident_bf[:, :], causal[:, :], start=False, stop=False)
                        pe.matmul(dst, ones_r[:, :], dsel[:, 0, 0:w], start=False, stop=False)
                        mm = pe.matmul(dst, ones_r[:, :], dsel[:, 1, 0:w], start=False, stop=True)
                mm.then_inc(s_mm, 1)

            def transposes(jj, head):
                pe.wait_ge(p_done, jj * 2 + (head + 1))
                for kb in range(QB):
                    for qb in range(kb, QB):
                        mm = pe.transpose(T_AT[kb][:, P * (qb - kb):P * (qb - kb) + P],
                                          prob[:, P_AT[qb] + P * kb:P_AT[qb] + P * kb + P], ident[:, :])
                mm.then_inc(t_mm, 1)

            def values(jj, head):
                hd = jj * 2 + head
                pe.wait_ge(pt_done, (hd + 1) * 3)
                wait(pe, o_done, hd)
                for kb in range(QB):
                    c, w = PT_AT[kb], T - P * kb
                    mm = passes(PV_BANK[:, P * kb:T], v_hi[:, kb, :], v_lo[:, kb, :],
                                pt_hi[:, c:c + w], pt_lo[:, c:c + w], kb == 0, kb == QB - 1)
                mm.then_inc(pv_mm, 1)

            def fox_step(a, j, jj, kk, before=None, after_q=None, fill=None):
                if j is not None:
                    slot(a, hh, hl, KT, before)
                if after_q:
                    after_q()
                if kk is not None:
                    values(kk, 1)
                if jj is not None:
                    pe.wait_ge(vt_done, jj + 1)
                    if kk is None:
                        pe.wait_ge(z_ready, 1)
                    for tb in range(QB):
                        mm = pe.transpose(V_BANK[:, P * tb:P * tb + P], vt[:, P * tb:P * tb + P], ident[:, :])
                    mm.then_inc(vt_mm, 1)
                    scores(jj, 0)
                    if fill:
                        fill(0)
                if j is not None:
                    slot(a + 1, hh, hl, KT)
                if jj is not None:
                    pe.wait_ge(v_done, jj + 1)
                    transposes(jj, 0)
                if j is not None:
                    slot(a + 2, hh, hl, KT)
                if jj is not None:
                    values(jj, 0)
                    scores(jj, 1)
                    if fill:
                        fill(1)
                if j is not None:
                    slot(a + 3, hh, hl, KT)
                if jj is not None:
                    transposes(jj, 1)
                if j is not None:
                    for t in range(2):
                        pe.wait_ge(sqh_done, j * 2 + (t + 1))
                        pe.matmul(HS_BANK[t][:, :], blk64[:, :], sq[:, t, :], start=True, stop=True).then_inc(hs_mm, 1)

            def forget_logits():
                pe.wait_ge(wf_split, 2)
                for k in range(KT):
                    mm = passes(bank[5][:, :], wf_hi[:, k, :], wf_lo[:, k, :], hh[:, k, :], hl[:, k, :],
                                k == 0, k == KT - 1)
                mm.then_inc(f_mm, 1)

            pe.wait_ge(ident_done, 1)
            fox_step(At(S_FOX), 0, None, None, first_input(1), forget_logits)
            fox_step(At(S_FOX + 4), 1, 0, None)
            with pe.Fori(1, KT - 1) as i:
                fox_step(At(S_FOX + 4, i, 4), i + 1, i, i - 1)

            def o_input(k):
                pe.wait_ge(o_done, 2 * (k + 1))

            def begin_out(head):
                slot(At(S_FOXO + head), hid_hi, hid_lo, KT, o_input, end=KT - 2)
            fox_step(None, None, KT - 1, KT - 2, fill=begin_out)
            fox_step(None, None, None, KT - 1)
            for head in range(2):
                slot(At(S_FOXO + head), hid_hi, hid_lo, KT, o_input, first=KT - 2)
            run(S_FOXO + 2, KT - 2, hid_hi, hid_lo, KT)
            boundary(2)
            ffn(2, S_UP2A, 2 * HH, tables=True)
            boundary(3)
            def by_half(g):
                return 4 * (g % 2) + g // 2

            def block_products(i, p):
                pe.wait_ge(ub_in[p], (i - p) * 64 + 128)
                pe.wait_ge(w1_in[p], (i - p) * 8 + 16)
                pe.wait_ge(w3_in[p], (i - p) * 8 + 16)
                wait(pe, blk_done, i * 3)
                for g in range(8):
                    u = ub[p][:, NBLK * g:NBLK * (g + 1)]
                    for t in range(2):
                        c = 4 * NBLK * t + NBLK * (g // 2)
                        pe.matmul(bank[6][rows(g), c:c + NBLK], w1[:, p, t, g // 2, rows(g)], u, start=True, stop=True)
                for g in range(8):
                    mm = pe.matmul(bank[7][:, NBLK * g:NBLK * (g + 1)], w3[:, p, by_half(g), :],
                                   ub[p][:, NBLK * g:NBLK * (g + 1)], start=True, stop=True)
                mm.then_inc(blk_mm, 1)

            def in_step(i, p, a):
                slot(a, hh, hl, KT, first_input(3) if isinstance(i, int) and i == 0 else None)
                if not isinstance(i, int) or i:
                    block_products(i - 1, 1 - p)
            by_tile(pe, 2, S_S5I, in_step)
            block_products(KT - 1, (KT - 1) % 2)

            def out_step(i, p, a):
                if i in (0, KT - 2):
                    pe.wait_ge(q2_in[i // (KT - 2)], 16)
                pe.wait_ge(xc_done, (i + 1) * 2)
                if not isinstance(i, int) or i >= 2:
                    pe.wait_ge(yb_done, i - 1)
                for g in range(8):
                    for t in range(2):
                        c = NBLK * (4 * t + g // 2)
                        mm = pe.matmul(bank[4 + 2 * p + g % 2][:, NBLK * (g // 2):NBLK * (g // 2 + 1) - 1],
                                       q2[rows(g), i, t, g // 2, CH:QW], sq[rows(g), p, c:c + NBLK - 1],
                                       start=t == 0, stop=t == 1)
                mm.then_inc(out_mm, 1)

            pe.wait_ge(blk_done, 3 * KT)
            for i in range(KT):
                out_step(i, i % 2, None)

            def glu_input(k):
                pe.wait_ge(h_done, 5 * KT + k + 1)

            def z_input(k):
                pe.wait_ge(z_done, k + 1)
            run(S_GLU, KT, hh, hl, KT, glu_input)
            run(S_S5O, KT, hid_hi, hid_lo, KT, z_input)
            boundary(4)
            ffn(4, S_UP3A, 4 * HH)
            boundary(5)



def tiles(w):
    k, m = w.shape
    return np.ascontiguousarray(w.reshape(k // P, P, m // P, P).transpose(2, 1, 0, 3).reshape(m // P, P, k))


def columns(v):
    return v.reshape(-1, P).T


def features(a):
    return np.ascontiguousarray(a.T.reshape(-1, P, a.shape[0]).transpose(1, 0, 2))


def up_tiles(gate, val):
    return np.ascontiguousarray(np.stack([tiles(gate), tiles(val)], 1).reshape(2 * HT, P, D))


def down_tiles(w):
    h = FF // 2
    return np.concatenate([tiles(w[:h]), tiles(w[h:])])


def layout(**a):
    o = {}
    vecs = {"mix_pre_g": a["mix_pre_g"][0], "mix_post_g": a["mix_post_g"][0], "ffn_pre_g": a["ffn_pre_g"][0],
            "ffn_post_g": a["ffn_post_g"][0], "pool_scale": a["pool_scale"][0],
            "s5_d": a["s5_d_2"][0]}
    for i in range(2):
        vecs[f"mix_pre_{i}"] = a["mix_pre_gain_2"][i]
        vecs[f"mix_post_{i}"] = a["mix_post_gain_2"][i]
        vecs[f"ffn_pre_{i}"] = a["ffn_pre_gain_2"][i]
        vecs[f"ffn_post_{i}"] = a["ffn_post_gain_2"][i]
    gains = [np.concatenate([a[n][0], a[n][0]])[:, None] for n in ("fox_q_gain_2", "fox_k_gain_2")]
    o["vec"] = np.ascontiguousarray(np.concatenate(
        [columns(vecs[n]) for n in VECS] + [columns(a["ada_b"][0])] + gains, axis=1))
    cw = np.concatenate([a["ffn_conv_w"][0], a["ffn_conv_b"]])
    o["convw"] = np.ascontiguousarray(cw.reshape(4, 2, HT, P).transpose(3, 2, 1, 0).reshape(P, HT, 8))
    o["x"] = features(a["x"][0])
    t = np.arange(T)
    o["rcnt"] = np.stack([1.0 / (np.minimum(t + w // 2, T) - np.maximum(t - w // 2, 0)) for w in WINDOWS]
                         ).astype(np.float32)
    o["ada_w"] = np.ascontiguousarray(a["ada_w"][0].T.reshape(24, 2, P, D).transpose(0, 2, 1, 3).reshape(24, P, 2 * D))
    o["c"] = np.ascontiguousarray(a["c"])
    pw = a["pool_w"][0].reshape(2, 2, 2, P, 2 * P)
    o["pool_w"] = np.ascontiguousarray(pw.transpose(0, 3, 1, 2, 4).reshape(2, P, WK))
    up = a["ffn_w_up"][0]
    o["up1"] = up_tiles(up[:, :FF], up[:, FF:])
    o["dn1"] = down_tiles(a["ffn_w_down"][0])
    fi = a["fox_w_in_2"][0]
    four = np.stack([tiles(fi[:, i * D:(i + 1) * D]) for i in range(4)], 1)
    o["fox_in"] = np.ascontiguousarray(four.reshape(4 * KT, P, D))
    o["fox_f"] = np.ascontiguousarray(fi[:, 4 * D:].reshape(KT, P, HEADS).transpose(1, 0, 2))
    o["fox_bf"] = np.ascontiguousarray(a["fox_b_f_2"][0][:, None])
    o["fox_out"] = tiles(a["fox_w_out_2"][0])
    for n in ("lam_re", "lam_im"):
        o[f"s5_{n}"] = np.ascontiguousarray(a[f"s5_{n}_2"][0].reshape(PAIRS, 2, STATE).transpose(1, 2, 0)
                                            .reshape(P, PAIRS))
    o["s5_log_dt"] = np.ascontiguousarray(a["s5_log_dt_2"][0].reshape(PAIRS, 2).T)
    b = np.stack([a["s5_b_re_2"][0], a["s5_b_im_2"][0]])
    o["s5_b"] = np.ascontiguousarray(b.reshape(2, PAIRS, 2, STATE, CH).transpose(2, 3, 0, 1, 4)
                                     .reshape(P, 2, PAIRS, CH))
    c = np.stack([a["s5_c_re_2"][0], a["s5_c_im_2"][0]])
    o["s5_c"] = np.ascontiguousarray(c.reshape(2, PAIRS, 2, CH, STATE).transpose(2, 4, 0, 1, 3)
                                     .reshape(P, 2, PAIRS, CH))
    o["s5_w"] = np.concatenate([tiles(a[f"s5_w_{n}_2"][0]) for n in ("in", "glu", "out")])
    for i in range(2):
        o[f"up{i + 2}"] = up_tiles(a["ffn_w_gate_2"][i], a["ffn_w_up_2"][i])
        o[f"dn{i + 2}"] = down_tiles(a["ffn_w_down_2"][i])
    return o


def kernel(**inputs):
    import concourse.bacc as bacc
    from concourse.bass_utils import run_bass_kernel_spmd

    arrays = layout(**{k: np.asarray(v) for k, v in inputs.items()})
    nc = bacc.Bacc("TRN2", target_bir_lowering=False, num_devices=1)
    dram = {n: nc.dram_tensor(f"in_{n}", v.shape, mybir.dt.from_np(v.dtype), kind="ExternalInput").ap()
            for n, v in arrays.items()}
    out = nc.dram_tensor("out", (P, KT, T), F32, kind="ExternalOutput").ap()
    build(nc, dram, out)
    r = run_bass_kernel_spmd(nc, [{f"in_{n}": v for n, v in arrays.items()}], core_ids=[0])
    got = np.asarray(r.results[0]["out"])
    return np.ascontiguousarray(got.transpose(1, 0, 2).reshape(D, T).T)[None]
```
